# Optimizing a Trainium2 kernel written in Bass

```python
import math
import jax, jax.numpy as jnp
from jax import lax
import numpy as np

D_MODEL = 2048
BATCH = 1
SEQ = 256
DEPTH = 1

N_META = 16
CONV_W = D_MODEL // 2
N_CONV_GROUPS = 16
CONV_K = 3
RWKV_W = D_MODEL // 2
HEAD_N = 64
N_RWKV_HEADS = RWKV_W // HEAD_N
DECAY_LORA = 96
AAA_LORA = 96
GATE_LORA = 256
D_FF = 5632
FFN_K = 3
RMS_EPS = 1e-6
GN_EPS = 64e-5
DECAY_SCALE = math.exp(-0.5)

CONV_COLS = 3 * CONV_W
RWKV_COLS = 3 * RWKV_W + DECAY_LORA + AAA_LORA + GATE_LORA
IN_COLS = CONV_COLS + RWKV_COLS


def rmsnorm(x, g):
    xf = x.astype(jnp.float32)
    y = xf * lax.rsqrt(jnp.mean(xf * xf, axis=-1, keepdims=True) + RMS_EPS)
    return (y * g.astype(jnp.float32)).astype(x.dtype)

def causal_dwconv(x, w):
    k = w.shape[0]
    seq_len = x.shape[1]
    xp = jnp.pad(x, ((0, 0), (k - 1, 0), (0, 0)))
    y = xp[:, 0:seq_len] * w[0]
    for i in range(1, k):
        y = y + xp[:, i:i + seq_len] * w[i]
    return y

def token_shift(z, mu):
    z_prev = jnp.pad(z, ((0, 0), (1, 0), (0, 0)))[:, :-1]
    return z + (z_prev - z) * mu

def rwkv7_scan(r, w, k, v, a_vec, b_vec):
    bsz, _, h, n = r.shape
    xs = tuple(jnp.swapaxes(t, 0, 1) for t in (r, w, k, v, a_vec, b_vec))

    def step(s, inp):
        r_t, w_t, k_t, v_t, a_t, b_t = inp
        sa = jnp.einsum('bhvk,bhk->bhv', s, a_t)
        s = s * w_t[:, :, None, :] + sa[..., None] * b_t[:, :, None, :] + v_t[..., None] * k_t[:, :, None, :]
        y_t = jnp.einsum('bhvk,bhk->bhv', s, r_t)
        return s, y_t

    s0 = jnp.zeros((bsz, h, n, n), jnp.float32)
    _, ys = lax.scan(step, s0, xs)
    return jnp.swapaxes(ys, 0, 1)

def short_conv_group(zc, conv_w):
    gate_b, gate_c, hx = jnp.split(zc, 3, axis=-1)
    return gate_b * causal_dwconv(gate_c * hx, conv_w)

def rwkv7_group(zr, mu_rwkv, w_decay_up, w0, a_up, a0, g_up, k_k, k_a, r_k, ln_x_w, ln_x_b):
    bsz, seq_len, _ = zr.shape
    zr = token_shift(zr, mu_rwkv)
    o1 = RWKV_W; o2 = 2 * RWKV_W; o3 = 3 * RWKV_W
    o4 = o3 + DECAY_LORA; o5 = o4 + AAA_LORA
    r = zr[..., :o1]
    k = zr[..., o1:o2]
    v = zr[..., o2:o3]
    wd = zr[..., o3:o4]
    ad = zr[..., o4:o5]
    gd = zr[..., o5:]

    f32 = jnp.float32
    log_w = -DECAY_SCALE * jax.nn.sigmoid((w0 + jnp.tanh(wd) @ w_decay_up).astype(f32))
    a = jax.nn.sigmoid(a0 + ad @ a_up)
    g = jax.nn.sigmoid(gd) @ g_up

    hs = (bsz, seq_len, N_RWKV_HEADS, HEAD_N)
    kk = (k * k_k).astype(f32).reshape(hs)
    kk = kk / jnp.maximum(jnp.sqrt(jnp.sum(kk * kk, axis=-1, keepdims=True)), 1e-12)
    k = k * (1.0 + (a - 1.0) * k_a)

    r_h = r.astype(f32).reshape(hs)
    k_h = k.astype(f32).reshape(hs)
    v_h = v.astype(f32).reshape(hs)
    a_h = a.astype(f32).reshape(hs)
    y = rwkv7_scan(r_h, jnp.exp(log_w).reshape(hs), k_h, v_h, -kk, kk * a_h)

    mean = jnp.mean(y, axis=-1, keepdims=True)
    var = jnp.mean(jnp.square(y - mean), axis=-1, keepdims=True)
    y = (y - mean) * lax.rsqrt(var + GN_EPS)
    y = y.reshape(bsz, seq_len, RWKV_W) * ln_x_w.astype(f32) + ln_x_b.astype(f32)
    bonus = jnp.sum(r_h * k_h * r_k.astype(f32), axis=-1, keepdims=True) * v_h
    y = y + bonus.reshape(bsz, seq_len, RWKV_W)
    return (y * g.astype(f32)).astype(zr.dtype)

def conv_glu(x, w_gate_up, conv_ffn, w_down):
    gu = x @ w_gate_up
    gate, up = jnp.split(gu, 2, axis=-1)
    gate = causal_dwconv(gate, conv_ffn)
    return (jax.nn.silu(gate) * up) @ w_down

def first_inputs(seed: int = 0) -> dict:
    key = jax.random.key(seed)
    ks = jax.random.split(key, 24)
    f32 = jnp.float32
    nrm = lambda k, shape, s: jax.random.normal(k, shape, f32) * s
    d = D_MODEL
    return {
        "x": nrm(ks[0], (BATCH, SEQ, d), 1.0),
        "meta_tokens": nrm(ks[1], (N_META, d), 1.0),
        "g_pre_mix": 1.0 + nrm(ks[2], (d,), 0.05),
        "w_in": nrm(ks[3], (d, IN_COLS), d ** -0.5),
        "conv_w": nrm(ks[4], (CONV_K, CONV_W), CONV_K ** -0.5),
        "mu_rwkv": jax.random.uniform(ks[5], (RWKV_COLS,), f32, 0.1, 0.9),
        "w_decay_up": nrm(ks[6], (DECAY_LORA, RWKV_W), 0.1 * DECAY_LORA ** -0.5),
        "w0": nrm(ks[7], (RWKV_W,), 0.5) - 0.5,
        "a_up": nrm(ks[8], (AAA_LORA, RWKV_W), 0.1 * AAA_LORA ** -0.5),
        "a0": nrm(ks[9], (RWKV_W,), 0.1),
        "g_up": nrm(ks[10], (GATE_LORA, RWKV_W), GATE_LORA ** -0.5),
        "k_k": 0.85 + nrm(ks[11], (RWKV_W,), 0.05),
        "k_a": 1.0 + nrm(ks[12], (RWKV_W,), 0.05),
        "r_k": nrm(ks[13], (N_RWKV_HEADS, HEAD_N), 0.1),
        "ln_x_w": 1.0 + nrm(ks[14], (RWKV_W,), 0.05),
        "ln_x_b": nrm(ks[15], (RWKV_W,), 0.02),
        "w_out": nrm(ks[16], (CONV_W + RWKV_W, d), (CONV_W + RWKV_W) ** -0.5),
        "g_post_mix": 1.0 + nrm(ks[17], (d,), 0.05),
        "g_pre_ffn": 1.0 + nrm(ks[18], (d,), 0.05),
        "w_gate_up": nrm(ks[19], (d, 2 * D_FF), d ** -0.5),
        "conv_ffn": nrm(ks[20], (FFN_K, D_FF), FFN_K ** -0.5),
        "w_down": nrm(ks[21], (D_FF, d), D_FF ** -0.5),
        "g_post_ffn": 1.0 + nrm(ks[22], (d,), 0.05),
    }

def first_block(x, meta_tokens, g_pre_mix, w_in, conv_w, mu_rwkv, w_decay_up, w0, a_up, a0,
              g_up, k_k, k_a, r_k, ln_x_w, ln_x_b, w_out, g_post_mix, g_pre_ffn,
              w_gate_up, conv_ffn, w_down, g_post_ffn):
    bsz = x.shape[0]
    meta = jnp.broadcast_to(meta_tokens.astype(x.dtype)[None], (bsz, N_META, x.shape[-1]))
    h = jnp.concatenate([meta, x], axis=1)

    for _ in range(DEPTH):
        n = rmsnorm(h, g_pre_mix)
        z = n @ w_in
        y_conv = short_conv_group(z[..., :CONV_COLS], conv_w)
        y_rwkv = rwkv7_group(z[..., CONV_COLS:], mu_rwkv, w_decay_up, w0, a_up, a0, g_up,
                             k_k, k_a, r_k, ln_x_w, ln_x_b)
        mix = jnp.concatenate([y_conv, y_rwkv], axis=-1) @ w_out
        h = h + rmsnorm(mix, g_post_mix)
        f = conv_glu(rmsnorm(h, g_pre_ffn), w_gate_up, conv_ffn, w_down)
        h = h + rmsnorm(f, g_post_ffn)

    return h[:, N_META:]


N_MIXERS = 4
HEAD_DIM = 64
N_HEADS = D_MODEL // HEAD_DIM
N_KV_HEADS = N_HEADS // 4
GQA_GROUP = N_HEADS // N_KV_HEADS
WINDOW = 128
Q_BLOCK = 128
DIFF_HEADS = D_MODEL // (2 * HEAD_DIM)
DIFF_V_DIM = 2 * HEAD_DIM
HGRN_HEAD_DIM = 128
HGRN_HEADS = D_MODEL // HGRN_HEAD_DIM
HGRN_CHUNK = 64
IDX_HEADS = 16
IDX_DIM = 64
TOPK_MAX = 256
CONV_WIDTH = 3
NUM_BUCKETS = 32
MAX_DISTANCE = 128
N_SWA = len(range(0, DEPTH, N_MIXERS))
N_DIFF = len(range(1, DEPTH, N_MIXERS))
N_HGRN = len(range(2, DEPTH, N_MIXERS))
N_DSA = len(range(3, DEPTH, N_MIXERS))
SWA_SPLITS = (N_HEADS * HEAD_DIM, N_KV_HEADS * HEAD_DIM, N_KV_HEADS * HEAD_DIM)
SWA_IN = sum(SWA_SPLITS)
DIFF_SPLITS = (DIFF_HEADS * 2 * HEAD_DIM, DIFF_HEADS * 2 * HEAD_DIM, DIFF_HEADS * DIFF_V_DIM)
DIFF_IN = sum(DIFF_SPLITS)
HGRN_IN = 4 * HGRN_HEADS * HGRN_HEAD_DIM
DSA_SPLITS = (N_HEADS * HEAD_DIM, N_KV_HEADS * HEAD_DIM, N_KV_HEADS * HEAD_DIM,
              IDX_HEADS * IDX_DIM, IDX_DIM, IDX_HEADS)
DSA_IN = sum(DSA_SPLITS)


def split_cols(z, sizes):
    return jnp.split(z, [int(c) for c in np.cumsum(sizes)[:-1]], axis=-1)

def rms_norm(x, g):
    xf = x.astype(jnp.float32)
    y = xf * lax.rsqrt(jnp.mean(xf * xf, axis=-1, keepdims=True) + RMS_EPS)
    return (y * g.astype(jnp.float32)).astype(x.dtype)

def rel_position_bias(dist, table):
    n = jnp.maximum(dist, 0)
    max_exact = NUM_BUCKETS // 2
    log_ratio = jnp.log(jnp.maximum(n, 1).astype(jnp.float32) / max_exact) / math.log(MAX_DISTANCE / max_exact)
    large = jnp.minimum(max_exact + (log_ratio * (NUM_BUCKETS - max_exact)).astype(jnp.int32), NUM_BUCKETS - 1)
    bucket = jnp.where(n < max_exact, n, large)
    return table.astype(jnp.float32)[bucket]

def swa_sink_attention(h, w_in, w_out, sinks, bias_table):
    B, S, _ = h.shape
    nb = S // Q_BLOCK
    q, k, v = split_cols(h @ w_in, SWA_SPLITS)
    q = q.reshape(B, nb, Q_BLOCK, N_KV_HEADS, GQA_GROUP, HEAD_DIM)
    pad = ((0, 0), (Q_BLOCK, 0), (0, 0))
    kp = jnp.pad(k, pad).reshape(B, nb + 1, Q_BLOCK, N_KV_HEADS, HEAD_DIM)
    vp = jnp.pad(v, pad).reshape(B, nb + 1, Q_BLOCK, N_KV_HEADS, HEAD_DIM)
    kb = jnp.concatenate([kp[:, :-1], kp[:, 1:]], axis=2)
    vb = jnp.concatenate([vp[:, :-1], vp[:, 1:]], axis=2)
    qi = jnp.arange(Q_BLOCK)
    kj = jnp.arange(2 * Q_BLOCK) - Q_BLOCK
    dist = qi[:, None] - kj[None, :]
    in_band = (dist >= 0) & (dist < WINDOW)
    key_exists = (jnp.arange(nb)[:, None] > 0) | (kj[None, :] >= 0)
    mask = in_band[None] & key_exists[:, None, :]
    bias = rel_position_bias(dist, bias_table).transpose(2, 0, 1).reshape(
        N_KV_HEADS, GQA_GROUP, Q_BLOCK, 2 * Q_BLOCK)
    s = jnp.einsum('bnqhgd,bnshd->bnhgqs', q, kb).astype(jnp.float32) * HEAD_DIM ** -0.5 + bias
    s = jnp.where(mask[None, :, None, None], s, -jnp.inf)
    sink = jnp.broadcast_to(sinks.astype(jnp.float32).reshape(N_KV_HEADS, GQA_GROUP, 1, 1),
                            s.shape[:-1] + (1,))
    p = jax.nn.softmax(jnp.concatenate([s, sink], axis=-1), axis=-1)[..., :-1]
    o = jnp.einsum('bnhgqs,bnshd->bnqhgd', p.astype(vb.dtype), vb)
    return o.reshape(B, S, N_HEADS * HEAD_DIM) @ w_out

def diff_attention(h, w_in, w_out, lambdas, subln_g, bias_table, layer_idx):
    B, S, _ = h.shape
    nb = S // Q_BLOCK
    q, k, v = split_cols(h @ w_in, DIFF_SPLITS)
    q = q.reshape(B, nb, Q_BLOCK, DIFF_HEADS, 2, HEAD_DIM).transpose(1, 0, 2, 3, 4, 5)
    k = k.reshape(B, S, DIFF_HEADS, 2, HEAD_DIM)
    v = v.reshape(B, S, DIFF_HEADS, DIFF_V_DIM)
    lam_init = 0.8 - 0.6 * math.exp(-0.3 * layer_idx)
    lf = lambdas.astype(jnp.float32)
    lam = jnp.exp(jnp.sum(lf[0] * lf[1])) - jnp.exp(jnp.sum(lf[2] * lf[3])) + lam_init
    kpos = jnp.arange(S)

    def block(args):
        qb, start = args
        dist = (start + jnp.arange(Q_BLOCK))[:, None] - kpos[None, :]
        bias = rel_position_bias(dist, bias_table).reshape(Q_BLOCK, S, DIFF_HEADS, 2).transpose(2, 3, 0, 1)
        s = jnp.einsum('bqhmd,bshmd->bhmqs', qb, k).astype(jnp.float32) * HEAD_DIM ** -0.5 + bias
        p = jax.nn.softmax(jnp.where(dist >= 0, s, -jnp.inf), axis=-1)
        a = p[:, :, 0] - lam * p[:, :, 1]
        return jnp.einsum('bhqs,bshe->bqhe', a.astype(v.dtype), v)

    o = lax.map(block, (q, jnp.arange(nb) * Q_BLOCK))
    o = o.transpose(1, 0, 2, 3, 4).reshape(B, S, DIFF_HEADS, DIFF_V_DIM)
    o = rms_norm(o, subln_g) * (1.0 - lam_init)
    return o.reshape(B, S, DIFF_HEADS * DIFF_V_DIM) @ w_out

def hgrn2_recurrence(h, w_in, w_out, lb, norm_g):
    B, S, _ = h.shape
    nc = S // HGRN_CHUNK
    f32 = jnp.float32
    q, fz, i, g = jnp.split(h @ w_in, 4, axis=-1)

    def chunks(t):
        return t.astype(f32).reshape(B, nc, HGRN_CHUNK, HGRN_HEADS, HGRN_HEAD_DIM).transpose(1, 0, 3, 2, 4)

    lbf = lb.astype(f32)
    log_f = jnp.logaddexp(jnp.log(lbf), jnp.log1p(-lbf) + jax.nn.log_sigmoid(fz.astype(f32)))
    key = -jnp.expm1(log_f)
    qs, ks, vs, gs = chunks(jax.nn.silu(q.astype(f32))), chunks(key), chunks(i), chunks(log_f)
    causal = jnp.tril(jnp.ones((HGRN_CHUNK, HGRN_CHUNK), dtype=bool))

    def step(state, inp):
        qc, kc, vc, gc = inp
        b = jnp.cumsum(gc, axis=2)
        o_inter = jnp.einsum('bhtk,bhkv->bhtv', qc * jnp.exp(b), state)
        rel = jnp.where(causal[:, :, None], b[:, :, :, None, :] - b[:, :, None, :, :], -jnp.inf)
        att = jnp.einsum('bhtsk,bhsk->bhts', qc[:, :, :, None, :] * jnp.exp(rel), kc)
        o_intra = jnp.einsum('bhts,bhsv->bhtv', att, vc)
        b_end = b[:, :, -1:, :]
        state = state * jnp.exp(b_end[:, :, 0, :, None]) + jnp.einsum(
            'bhsk,bhsv->bhkv', kc * jnp.exp(b_end - b), vc)
        return state, o_inter + o_intra

    state0 = jnp.zeros((B, HGRN_HEADS, HGRN_HEAD_DIM, HGRN_HEAD_DIM), f32)
    _, o = lax.scan(step, state0, (qs, ks, vs, gs))
    o = o.transpose(1, 0, 3, 2, 4).reshape(B, S, HGRN_HEADS, HGRN_HEAD_DIM)
    gate = jax.nn.silu(g.astype(f32)).reshape(B, S, HGRN_HEADS, HGRN_HEAD_DIM)
    o = (rms_norm(o, norm_g) * gate).astype(h.dtype)
    return o.reshape(B, S, HGRN_HEADS * HGRN_HEAD_DIM) @ w_out

def dsa_sparse_attention(h, w_in, w_out, bias_table):
    B, S, _ = h.shape
    nb = S // Q_BLOCK
    n_sel = min(TOPK_MAX, S // 4)
    f32 = jnp.float32
    q, k, v, qi, ki, wi = split_cols(h @ w_in, DSA_SPLITS)
    q = q.reshape(B, nb, Q_BLOCK, N_KV_HEADS, GQA_GROUP, HEAD_DIM).transpose(1, 0, 2, 3, 4, 5)
    qi = qi.reshape(B, nb, Q_BLOCK, IDX_HEADS, IDX_DIM).transpose(1, 0, 2, 3, 4)
    wi = wi.reshape(B, nb, Q_BLOCK, IDX_HEADS).transpose(1, 0, 2, 3)
    k = k.reshape(B, S, N_KV_HEADS, HEAD_DIM)
    v = v.reshape(B, S, N_KV_HEADS, HEAD_DIM)
    kpos = jnp.arange(S)
    gather = jax.vmap(lambda t, idx: t[idx])

    def block(args):
        qb, qib, wib, start = args
        qpos = start + jnp.arange(Q_BLOCK)
        logits = jnp.einsum('bqhd,bsd->bqhs', qib, ki).astype(f32) * IDX_DIM ** -0.5
        score = jnp.einsum('bqh,bqhs->bqs', wib.astype(f32) * IDX_HEADS ** -0.5, jax.nn.relu(logits))
        score = jnp.where(qpos[:, None] >= kpos[None, :], score, -jnp.inf)
        _, idx = lax.top_k(score, n_sel)
        valid = idx <= qpos[None, :, None]
        kg, vg = gather(k, idx), gather(v, idx)
        s = jnp.einsum('bqhgd,bqkhd->bhgqk', qb, kg).astype(f32) * HEAD_DIM ** -0.5
        bias = rel_position_bias(qpos[None, :, None] - idx, bias_table).transpose(0, 3, 1, 2).reshape(
            B, N_KV_HEADS, GQA_GROUP, Q_BLOCK, n_sel)
        s = jnp.where(valid[:, None, None], s + bias, -jnp.inf)
        p = jax.nn.softmax(s, axis=-1)
        return jnp.einsum('bhgqk,bqkhd->bqhgd', p.astype(vg.dtype), vg)

    o = lax.map(block, (q, qi, wi, jnp.arange(nb) * Q_BLOCK))
    return o.transpose(1, 0, 2, 3, 4, 5).reshape(B, S, N_HEADS * HEAD_DIM) @ w_out

def conv_ffn(h, w_up, conv_w, w_down):
    S = h.shape[1]
    u = h @ w_up
    up = jnp.pad(u, ((0, 0), (CONV_WIDTH - 1, 0), (0, 0)))
    c = conv_w[0] * up[:, 0:S]
    for j in range(1, CONV_WIDTH):
        c = c + conv_w[j] * up[:, j:j + S]
    gate, val = jnp.split(c, 2, axis=-1)
    return (jax.nn.silu(gate) * val) @ w_down

def second_inputs(seed: int = 0) -> dict:
    key = jax.random.key(seed)
    ks = jax.random.split(key, 20)
    f32 = jnp.float32

    def dense(k, shape, fan_in):
        return jax.random.normal(k, shape, f32) * fan_in ** -0.5

    return {
        'x': jax.random.normal(ks[0], (BATCH, SEQ, D_MODEL), f32),
        'rel_bias_table': 0.3 * jax.random.normal(ks[1], (NUM_BUCKETS, N_HEADS), f32),
        'hgrn_lb_logits': 0.5 * jax.random.normal(ks[2], (DEPTH, HGRN_HEADS * HGRN_HEAD_DIM), f32),
        'norm_g': 1.0 + 0.02 * jax.random.normal(ks[3], (DEPTH, 4, D_MODEL), f32),
        'ffn_w_up': dense(ks[4], (DEPTH, D_MODEL, 2 * D_FF), D_MODEL),
        'ffn_conv': dense(ks[5], (DEPTH, CONV_WIDTH, 2 * D_FF), CONV_WIDTH),
        'ffn_w_down': dense(ks[6], (DEPTH, D_FF, D_MODEL), D_FF),
        'swa_w_in': dense(ks[7], (N_SWA, D_MODEL, SWA_IN), D_MODEL),
        'swa_w_out': dense(ks[8], (N_SWA, N_HEADS * HEAD_DIM, D_MODEL), N_HEADS * HEAD_DIM),
        'swa_sinks': 0.5 * jax.random.normal(ks[9], (N_SWA, N_HEADS), f32),
        'diff_w_in': dense(ks[10], (N_DIFF, D_MODEL, DIFF_IN), D_MODEL),
        'diff_w_out': dense(ks[11], (N_DIFF, DIFF_HEADS * DIFF_V_DIM, D_MODEL), DIFF_HEADS * DIFF_V_DIM),
        'diff_lambda': 0.1 * jax.random.normal(ks[12], (N_DIFF, 4, HEAD_DIM), f32),
        'diff_subln_g': 1.0 + 0.02 * jax.random.normal(ks[13], (N_DIFF, DIFF_V_DIM), f32),
        'hgrn_w_in': dense(ks[14], (N_HGRN, D_MODEL, HGRN_IN), D_MODEL),
        'hgrn_w_out': dense(ks[15], (N_HGRN, HGRN_HEADS * HGRN_HEAD_DIM, D_MODEL), HGRN_HEADS * HGRN_HEAD_DIM),
        'hgrn_norm_g': 1.0 + 0.02 * jax.random.normal(ks[16], (N_HGRN, HGRN_HEAD_DIM), f32),
        'dsa_w_in': dense(ks[17], (N_DSA, D_MODEL, DSA_IN), D_MODEL),
        'dsa_w_out': dense(ks[18], (N_DSA, N_HEADS * HEAD_DIM, D_MODEL), N_HEADS * HEAD_DIM),
    }

def second_block(x, rel_bias_table, hgrn_lb_logits, norm_g, ffn_w_up, ffn_conv, ffn_w_down,
              swa_w_in, swa_w_out, swa_sinks, diff_w_in, diff_w_out, diff_lambda, diff_subln_g,
              hgrn_w_in, hgrn_w_out, hgrn_norm_g, dsa_w_in, dsa_w_out):
    lb_soft = jax.nn.softmax(hgrn_lb_logits.astype(jnp.float32), axis=0)
    lb_all = jnp.cumsum(lb_soft, axis=0) - lb_soft[0]
    for i in range(DEPTH):
        kind, j = i % N_MIXERS, i // N_MIXERS
        h = rms_norm(x, norm_g[i, 0])
        if kind == 0:
            m = swa_sink_attention(h, swa_w_in[j], swa_w_out[j], swa_sinks[j], rel_bias_table)
        elif kind == 1:
            m = diff_attention(h, diff_w_in[j], diff_w_out[j], diff_lambda[j], diff_subln_g[j],
                               rel_bias_table, i)
        elif kind == 2:
            m = hgrn2_recurrence(h, hgrn_w_in[j], hgrn_w_out[j], lb_all[i], hgrn_norm_g[j])
        else:
            m = dsa_sparse_attention(h, dsa_w_in[j], dsa_w_out[j], rel_bias_table)
        x = x + rms_norm(m, norm_g[i, 1])
        h = rms_norm(x, norm_g[i, 2])
        x = x + rms_norm(conv_ffn(h, ffn_w_up[i], ffn_conv[i], ffn_w_down[i]), norm_g[i, 3])
    return x


def setup_inputs(seed=0):
    out = dict(first_inputs(seed))
    for name, value in second_inputs(seed + 1).items():
        if name != "x":
            out[name + "_2"] = value
    return out


def reference(
    x, meta_tokens, g_pre_mix, w_in, conv_w, mu_rwkv, w_decay_up, w0, a_up, a0, g_up, k_k, k_a,
    r_k, ln_x_w, ln_x_b, w_out, g_post_mix, g_pre_ffn, w_gate_up, conv_ffn, w_down, g_post_ffn,
    rel_bias_table_2, hgrn_lb_logits_2, norm_g_2, ffn_w_up_2, ffn_conv_2, ffn_w_down_2,
    swa_w_in_2, swa_w_out_2, swa_sinks_2, diff_w_in_2, diff_w_out_2, diff_lambda_2,
    diff_subln_g_2, hgrn_w_in_2, hgrn_w_out_2, hgrn_norm_g_2, dsa_w_in_2, dsa_w_out_2,
):
    x = first_block(
        x, meta_tokens, g_pre_mix, w_in, conv_w, mu_rwkv, w_decay_up, w0, a_up, a0, g_up, k_k,
        k_a, r_k, ln_x_w, ln_x_b, w_out, g_post_mix, g_pre_ffn, w_gate_up, conv_ffn, w_down,
        g_post_ffn,
    )
    return second_block(
        x, rel_bias_table_2, hgrn_lb_logits_2, norm_g_2, ffn_w_up_2, ffn_conv_2, ffn_w_down_2,
        swa_w_in_2, swa_w_out_2, swa_sinks_2, diff_w_in_2, diff_w_out_2, diff_lambda_2,
        diff_subln_g_2, hgrn_w_in_2, hgrn_w_out_2, hgrn_norm_g_2, dsa_w_in_2, dsa_w_out_2,
    )


_drawn_inputs = setup_inputs


def setup_inputs(seed=0):
    import zlib

    import numpy as np

    out = dict(_drawn_inputs(seed))
    spreads = {}
    factors = {'w_decay_up': 8.0, 'k_k': 7.489, 'ln_x_b': 3.223, 'swa_sinks_2': 5.346}
    for name, (base, spread) in spreads.items():
        noise = np.random.default_rng([zlib.crc32(name.encode()), seed]).standard_normal(out[name].shape)
        drawn = base * np.exp(spread * noise) if base else spread * noise
        out[name] = __import__('jax').numpy.asarray(drawn.astype(out[name].dtype))
    for name, factor in factors.items():
        out[name] = (out[name] * factor).astype(out[name].dtype)
    return out
```

```python
import math
from contextlib import ExitStack

import numpy as np

import concourse.bass as bass
from concourse import mybir

F32 = mybir.dt.float32
F32R = mybir.dt.float32r
ALU = mybir.AluOpType
ACT = mybir.ActivationFunctionType

P = 128
D = 2048
KT = D // P
SEQ = 256
N_META = 16
L = SEQ + N_META
D_FF = 5632
FT = D_FF // P
RW = D // 2
RT = RW // P
HEAD = 64
LORA = 96
N_HEADS = 32
QB = 128
DECAY_SCALE = math.exp(-0.5)
RMS_EPS = 1e-6
GN_EPS = 64e-5
MASKED = -1e30

LG = SEQ + 2
TG = L - LG
TU = L - SEQ

PROJECTIONS = [("w_in", 13, 8), ("w_out", 4, 8), ("gate_up", 22, 8), ("down", 4, 22),
               ("in2", 6, 8), ("out2", 4, 8), ("up2", 22, 8), ("down2", 4, 22)]
FIRST, GROUPS, CHUNKS = {}, {}, {}
_n = 0
for _name, _g, _c in PROJECTIONS:
    FIRST[_name], GROUPS[_name], CHUNKS[_name] = _n, _g, _c
    _n += _g * _c
N_CHUNKS = _n
RING = 4

VEC = {}
_n = 0
for _name, _w in [("g_pre_mix", KT), ("g_post_mix", KT), ("g_pre_ffn", KT), ("g_post_ffn", KT),
                  ("norm0", KT), ("norm1", KT), ("norm2", KT), ("norm3", KT), ("mu", 28), ("w0", RT),
                  ("a0", RT), ("k_k", RT), ("k_a", RT), ("r_k", RT), ("ln_w", RT), ("ln_b", RT),
                  ("conv_w", 3 * RT), ("conv_ffn", 3 * FT), ("conv_ffn2", 6 * FT)]:
    VEC[_name] = _n
    _n += _w
N_VEC = _n

C = 64
CHUNK_LENGTHS = [64, 64, 64, 64, 16]
LEVELS = [6, 6, 6, 6, 4]


class Count:

    def __init__(self):
        self.n = 0

    def add(self):
        self.n = self.n + 1
        return self.n

    def enter(self, i, first, per_turn):
        self.start, self.per_turn = self.n, per_turn
        self.n = i * per_turn + (self.n - first * per_turn)

    def leave(self, turns):
        self.n = self.start + turns * self.per_turn


def program(nc, d):
    with ExitStack() as ctx:
        def sem(name):
            return ctx.enter_context(nc.semaphore(name))

        base = [0]

        def at(name, shape, dt, offset):
            with ExitStack() as s:
                if offset:
                    s.enter_context(nc.sbuf_tensor(name + "_below", [P, offset // 4], F32))
                return s.enter_context(nc.sbuf_tensor(name, shape, dt))

        def persistent(name, shape, dt=F32):
            t = at(name, shape, dt, base[0])
            size = 4 * int(np.prod(shape[1:]))
            base[0] += -(-size // 32) * 32
            return t

        raw = persistent("raw", [P, RING, 2, 512])
        wh = persistent("wh", [P, RING, 2, 512], F32R)
        wl = persistent("wl", [P, RING, 2, 512], F32R)
        vec = persistent("vec", [P, N_VEC])
        ident = persistent("ident", [P, P])
        ones = persistent("ones", [P, P])
        bones = persistent("bones", [P, P])
        rstd = persistent("rstd", [P, L])
        rstd_post = persistent("rstd_post", [P, L])
        LENT = base[0] - 4 * L
        sq = persistent("sq", [P, 2, L])
        sq_sum = persistent("sq_sum", [P, L])
        scaled = persistent("scaled", [P, 2, L])
        mean_sq = persistent("mean_sq", [P, L])
        root = persistent("root", [P, L])
        R = base[0]

        def region(name, shape, offset, dt=F32):
            return at(name, shape, dt, R + offset)

        h = region("h", [P, KT, L], 0)
        xh = region("xh", [P, KT, L], 17408, F32R)
        xl = region("xl", [P, KT, L], 34816, F32R)
        z = region("z", [P, 28, L + 1], 52224)
        ych = region("ych", [P, RT, LG], 82816, F32R)
        ycl = region("ycl", [P, RT, LG], 91072, F32R)
        cg = region("cg", [P, 4, LG + 2], 99328)
        hg = region("hg", [P, 4, LG + 2], 103488)
        cc = region("cc", [P, 4, LG], 107648)
        bg = region("bg", [P, 4, LG], 111776)
        zd = region("zd", [P, 4, L], 115904)
        wdu = region("wdu", [LORA, RW], 120320)
        aup = region("aup", [LORA, RW], 124416)
        gup = region("gup", [P, 2, RW], 128512)
        rkr = region("rkr", [P, RT, L], 136704)
        tw = region("tw", [P, L], 145408)
        sgd = region("sgd", [P, 2, L], 146496)
        reset = region("reset", [P, L], 148672)
        table = region("table", [32, N_HEADS], 149760)
        onehot = region("onehot", [32, 384], 149888)
        maskrow = region("maskrow", [32, 384], 151424)
        erow = region("erow", [32, 384], 152960)
        lmask = region("lmask", [P, 6, P], 160768)
        gmask = region("gmask", [P, 2, C], 163840)
        b_ = region("b", [P, RT, L], 0)
        kn = region("kn", [P, RT, L], 8704)
        cum = region("cum", [P, RT, L], 17408)
        bonus = region("bonus", [P, RT, L], 26112)
        gate = region("gate", [P, RT, L], 34816)
        pe1 = region("pe1", [P, RT, C + 1], 43520)
        pinv = region("pinv", [P, RT, C], 45600)
        sw = region("sw", [P, RT, L], 99328)
        kksq = region("kksq", [P, RT, L], 108032)
        _o = [99328]

        def chunk_buffer(name, width=P):
            t = region(name, [P, RT, width], _o[0])
            _o[0] += 4 * RT * width
            return t

        HALF_TILES = RT // 2
        ar = [chunk_buffer("ar0", 2 * P), chunk_buffer("ar1", 2 * P)]
        bkf, bkt = chunk_buffer("bkf"), chunk_buffer("bkt")
        xuv = [chunk_buffer("xuv0"), chunk_buffer("xuv1")]
        ga = chunk_buffer("ga")
        gr = [chunk_buffer("gr0"), chunk_buffer("gr1")]
        tt = chunk_buffer("tt")
        am = [chunk_buffer("am0"), chunk_buffer("am1")]
        st = chunk_buffer("st")
        tn = at("tn", [P, RT, P], F32, LENT)
        qb = at("qb", [P, RT, P], F32, LENT + 4 * RT * P)
        vd = region("vd", [P, RT, P], 47648)
        zb = region("zb", [P, RT, P], 52224)
        pend = region("pend", [P, len(CHUNK_LENGTHS), RT], 164352)
        yrh = region("yrh", [P, RT, LG], 99328, F32R)
        yrl = region("yrl", [P, RT, LG], 107584, F32R)
        yc = region("yc", [P, RT, LG], 17408)
        yc2 = region("yc2", [P, RT, LG], 0)
        mix = region("mix", [P, KT, LG], 116000)
        gt = region("gt", [P, 4, LG], 52224)
        cv = region("cv", [P, 4, SEQ], 56352)
        sg = region("sg", [P, 4, SEQ], 60448)
        ut = region("ut", [P, 4, SEQ], 64544)
        av = region("av", [P, 4, SEQ], 68640)
        acth = region("acth", [P, FT, SEQ], 73216, F32R)
        actl = region("actl", [P, FT, SEQ], 118272, F32R)
        mixf = region("mixf", [P, KT, SEQ], 52224)
        qf = region("qf", [P, KT, SEQ], 52224)
        kf = region("kf", [P, 4, SEQ], 68608)
        vf = region("vf", [P, 4, SEQ], 72704)
        vt = region("vt", [P, 2, 512], 76800)
        bias = region("bias", [P, N_HEADS, SEQ], 80896)
        y2h = region("y2h", [P, KT, SEQ], 113664, F32R)
        y2l = region("y2l", [P, KT, SEQ], 130048, F32R)
        SLOTS = 4
        sc = region("sc", [P, SLOTS, 384], 146432)
        pr = region("pr", [P, SLOTS, 384], 152576)
        pt = region("pt", [P, 2, 3, 4, QB], 17408)
        _o = [R + 164864]
        stats = []
        for name in ("rowmax", "negmax", "rowsum", "esink", "denom", "rdenom"):
            stats.append(at(name, [P, SLOTS, 2], F32, _o[0]))
            _o[0] += 32
        rowmax, negmax, rowsum, esink, denom, rdenom = stats
        sinks = at("sinks", [P, N_HEADS], F32, _o[0])
        mix2 = region("mix2", [P, KT, SEQ], 52224)

        ps = ctx.enter_context(nc.psum_tensor("ps", [P, 8, 512], F32))

        landed = [sem(f"landed{i}") for i in range(RING)]
        high_ready, low_ready, chunk_used = sem("high_ready"), sem("low_ready"), sem("chunk_used")
        vec_landed, consts, h_landed, lora_landed = sem("vec_landed"), sem("consts"), sem("h_landed"), sem("lora_landed")
        bias_stored, bias_landed, erow_ready, sinks_landed = (sem("bias_stored"), sem("bias_landed"),
                                                              sem("erow_ready"), sem("sinks_landed"))
        bias_mm = sem("bias_mm")
        x_high, x_low, h_ready = sem("x_high"), sem("x_low"), sem("h_ready")
        sq_ready, sq_added = sem("sq_ready"), sem("sq_added")
        ss_done, ms_ready, root_ready, rstd_ready = sem("ss_done"), sem("ms_ready"), sem("root_ready"), sem("rstd_ready")
        group_read = sem("group_read")
        cv_ready, sg_ready, av_ready, act_high, act_low = (sem("cv_ready"), sem("sg_ready"), sem("av_ready"),
                                                           sem("act_high"), sem("act_low"))
        dve_step, z_edge_zero = sem("dve_step"), sem("z_edge_zero")
        yv_ready, y_high, y_low = sem("yv_ready"), sem("y_high"), sem("y_low")
        z_ready = sem("z_ready")
        stored = sem("stored")
        pre_act, pre_dve, pre_pe = sem("pre_act"), sem("pre_dve"), sem("pre_pe")
        exp_ready, fac_ready, bk_ready, vd_ready, zeroed = (sem("exp_ready"), sem("fac_ready"), sem("bk_ready"),
                                                            sem("vd_ready"), sem("zeroed"))
        gram_done, bk_turned, bkt_ready, v_done, v_ready = (sem("gram_done"), sem("bk_turned"), sem("bkt_ready"),
                                                            sem("v_done"), sem("v_ready"))
        am_ready, am_turned, q_done, q_ready, d_done, tt_ready = (sem("am_ready"), sem("am_turned"), sem("q_done"),
                                                                  sem("q_ready"), sem("d_done"), sem("tt_ready"))
        z_done, zb_ready, u_done, x_ready, s_done, st_ready, y_done, y_ready = (
            sem("z_done"), sem("zb_ready"), sem("u_done"), sem("x_ready"), sem("s_done"), sem("st_ready"),
            sem("y_done"), sem("y_ready"))
        v_turned, vt_ready = sem("v_turned"), sem("vt_ready")
        s_ready, sc_ready, max_ready, p_ready, pn_ready = (sem("s_ready"), sem("sc_ready"), sem("max_ready"),
                                                           sem("p_ready"), sem("pn_ready"))
        p_turned, pt_ready, o_done, o_high, o_low = (sem("p_turned"), sem("pt_ready"), sem("o_done"),
                                                     sem("o_high"), sem("o_low"))

        G0, n = {}, 0
        for name, groups, _ in PROJECTIONS:
            G0[name] = n
            n += groups

        scratch = nc.dram_tensor("bias_rows", [N_HEADS, 384], F32, kind="Internal").ap()

        def vcol(name, i):
            return vec[:, bass.ds(VEC[name] + i, 1)]

        def over(ap, tiles):
            return ap.unsqueeze(1).broadcast_to([ap.shape[0], tiles, ap.shape[1]])

        SUMS = [("w_in", L), ("w_out", LG), ("gate_up", LG), ("down", SEQ),
                ("in2", SEQ), ("out2", SEQ), ("up2", SEQ), ("down2", SEQ)]
        SUM = {name: s for s, (name, _) in enumerate(SUMS)}
        TOKENS = dict(SUMS)
        XSPLIT = {"w_in": 0, "gate_up": 1, "in2": 2, "up2": 3}
        PAIRS = D_FF // 512

        N_RC = len(CHUNK_LENGTHS)
        T0 = [sum(CHUNK_LENGTHS[:c]) for c in range(N_RC)]

        def nth(c, half=1):
            return 2 * c + half + 1

        def level(c, l, half=1):
            return 2 * (sum(LEVELS[:c]) + l) + half + 1

        def inner(c, l, half=1):
            return 2 * (sum(LEVELS[:c]) - c + l - 1) + half + 1

        def u_zero(c):
            return 4 * min(c + 1, 2) + 2 * max(c - 1, 0)

        def tiles(t, half):
            return t[:, HALF_TILES * half:HALF_TILES * (half + 1)]

        def bank(b):
            return ps[:, b, :].rearrange("p (f t) -> p f t", f=HALF_TILES)

        HEAD_ROWS = [slice(0, HEAD), slice(HEAD, P)]

        block = ctx.enter_context(nc.Block())

        @block.sync
        def _(sp):
            def load(weights, i, slot, index):
                sp.dma_start(raw[:, slot], weights[index]).then_inc(landed[slot], 16)

            for name, groups, chunks in PROJECTIONS:
                weights = d[name]
                first = FIRST[name]
                if first == 0:
                    for j in range(RING):
                        sp.dma_start(raw[:, j], weights[j]).then_inc(landed[j], 16)
                start = 1 if first == 0 else 0
                with sp.Fori(start, groups * chunks // RING) as i:
                    for j in range(RING):
                        sp.wait_ge(low_ready, i * RING + (first + j - RING + 1))
                        sp.dma_start(raw[:, j], weights[i * RING + j]).then_inc(landed[j], 16)
            for k in range(0, KT, 4):
                sp.wait_ge(h_ready, 16 * 3 + k + 4)
                sp.dma_start(d["out"][:, k:k + 4, :], h[:, k:k + 4, TU:L]).then_inc(stored, 16)
            sp.wait_ge(stored, 16 * 4)

        @block.gpsimd
        def _(pool):
            pool.memset(z[:, :, 0:1], 0.0).then_inc(z_edge_zero, 1)

            for s, (name, n) in enumerate(SUMS):
                def add(k, slot):
                    pool.wait_ge(sq_ready, 16 * s + k + 1)
                    pool.wait_ge(sq_added, 16 * s + k)
                    pool.tensor_tensor(sq_sum[:, 0:n], sq_sum[:, 0:n], sq[:, slot, 0:n], ALU.add).then_inc(sq_added, 1)

                pool.wait_ge(sq_ready, 16 * s + 1)
                if s:
                    pool.wait_ge(ss_done, s)
                pool.tensor_copy(sq_sum[:, 0:n], sq[:, 0, 0:n]).then_inc(sq_added, 1)
                add(1, 1)
                with pool.Fori(1, KT // 2) as i:
                    add(2 * i, 0)
                    add(2 * i + 1, 1)
                if s:
                    continue
                pool.wait_ge(pre_dve, 8)
                n_zeroed = 0
                for c, n in enumerate(CHUNK_LENGTHS):
                    t0, short = T0[c], n < C
                    if c >= 2:
                        pool.wait_ge(y_done, nth(c - 2))
                        pool.wait_ge(s_done, nth(c - 2))
                    for own in (True, False) if c < 2 else (True,):
                        for e in range(2):
                            if n_zeroed:
                                pool.wait_ge(zeroed, n_zeroed)
                            cols = slice(64 * e, 64 * e + 64) if own else slice(64 - 64 * e, 128 - 64 * e)
                            pool.memset(xuv[c % 2][HEAD_ROWS[e], :, cols], 0.0).then_inc(zeroed, 1)
                            n_zeroed += 1
                    if short:
                        pool.wait_ge(zeroed, u_zero(c))
                        pool.memset(ar[c % 2][:], 0.0).then_inc(zeroed, 1)
                        pool.wait_ge(zeroed, u_zero(c) + 1)
                    pool.wait_ge(exp_ready, 2 * c + 2)
                    if c:
                        pool.wait_ge(bk_turned, nth(c - 1))
                    if short:
                        pool.memset(bkf[:], 0.0).then_inc(zeroed, 1)
                    pool.wait_ge(zeroed, u_zero(c) + 2 * short)
                    for e in range(2):
                        rows = HEAD_ROWS[e]
                        pool.tensor_tensor(bkf[rows, :, 64 * e:64 * e + n], b_[rows, :, t0:t0 + n], pinv[rows, :, 0:n],
                                           ALU.mult).then_inc(bk_ready, 1)
                        pool.wait_ge(bk_ready, 4 * c + 2 * e + 1)
                        pool.tensor_tensor(bkf[rows, :, 64 - 64 * e:64 - 64 * e + n], z[rows, 12:20, 1 + t0:1 + t0 + n],
                                           pinv[rows, :, 0:n], ALU.mult).then_inc(bk_ready, 1)
                        pool.wait_ge(bk_ready, 4 * c + 2 * e + 2)
                    if short:
                        pool.wait_ge(v_done, nth(c - 1))
                        pool.memset(vd[:], 0.0).then_inc(zeroed, 1)

        @block.scalar
        def _(act):

            def high(n, slot):
                if not isinstance(n, int):
                    act.wait_ge(landed[slot], (n - slot) * (16 // RING) + 16)
                    act.wait_ge(chunk_used, n - (RING - 1))
                else:
                    act.wait_ge(landed[slot], 16 * (n // RING + 1))
                    if n >= RING:
                        act.wait_ge(chunk_used, n - RING + 1)
                act.activation(wh[:, slot], raw[:, slot], ACT.Copy).then_inc(high_ready, 1)

            def highs(first, count, slot=0):
                for c in range(count):
                    high(first + c, (slot + c) % RING)

            def clamp(first, count):
                return max(0, min(count, N_CHUNKS - first))

            def square(src, index, n):
                if index >= 2:
                    act.wait_ge(sq_added, index - 1)
                act.activation(sq[:, index % 2, 0:n], src, ACT.Square).then_inc(sq_ready, 1)

            def take_root(s, n):
                act.wait_ge(ms_ready, s + 1)
                act.activation(root[:, 0:n], mean_sq[:, 0:n], ACT.Sqrt).then_inc(root_ready, 1)

            def x_tile(name, k, t0, gain):
                n = TOKENS[name]
                act.activation(xh[:, k, 0:n], h[:, k, t0:t0 + n], ACT.Copy, scale=vcol(gain, k)).then_inc(x_high, 1)
                square(h[:, k, t0:t0 + n], 16 * SUM[name] + k, n)

            def opening(name, tile):
                first = FIRST[name]
                for c in range(8):
                    tile(2 * c)
                    tile(2 * c + 1)
                    if c >= 3:
                        highs(first + 4 + c - 3, 1, (c - 3) % RING)
                highs(first + 9, 3, 1)
                take_root(SUM[name], TOKENS[name])

            def mix_group(name, g, src, n):
                act.wait_ge(group_read, G0[name] + g + 1)
                for k in range(4 * g, 4 * g + 4):
                    square(src[:, k, :], 16 * SUM[name] + k, n)

            def plain(name, evacuate, skip_first=False):
                first, per = FIRST[name], CHUNKS[name]
                for g in range(1 if skip_first else 0, GROUPS[name]):
                    start = first + g * per + RING
                    count = clamp(start, per)
                    head = min(count, 1)
                    highs(start, head, start % RING)
                    if g:
                        evacuate(g - 1)
                    if count - head > 8:
                        more(start + head, count - head)
                    else:
                        highs(start + head, count - head, (start + head) % RING)
                evacuate(GROUPS[name] - 1)

            def more(first, count):
                slot = first % RING
                with act.Fori(0, count // RING) as i:
                    highs(i * RING + first, RING, slot)
                highs(first + count // RING * RING, count % RING, slot)

            act.dma_start(vec[:], d["vec"]).then_inc(vec_landed, 16)
            for k in range(0, KT, 4):
                act.dma_start(h[:, k:k + 4, :], d["ht"][:, k:k + 4, :]).then_inc(h_landed, 16)
            for dst, src in ((ident, "ident"), (ones, "ones"), (bones, "bones"), (table, "table"), (onehot, "onehot"),
                             (maskrow, "maskrow")):
                act.dma_start(dst[:], d[src]).then_inc(consts, 16)
            for dst, src in ((wdu, "wdu"), (aup, "aup"), (gup, "gup"), (reset, "reset"), (lmask, "lmask"),
                             (gmask, "gmask")):
                act.dma_start(dst[:], d[src]).then_inc(lora_landed, 16)
            act.wait_ge(vec_landed, 16)
            act.wait_ge(h_landed, 16 * 4)
            highs(0, 4)
            opening("w_in", lambda k: x_tile("w_in", k, 0, "g_pre_mix"))

            def evacuate_in(g):
                if g in (9, 12):
                    half = (g - 9) // 3
                    act.wait_ge(yv_ready, half + 1)
                    act.activation(ych[:, 4 * half:4 * half + 4], bg[:], ACT.Copy).then_inc(y_high, 1)

            plain("w_in", evacuate_in, skip_first=True)

            act.wait_ge(erow_ready, 1)
            act.dma_start(scratch, erow[:]).then_inc(bias_stored, 16)

            act.wait_ge(z_ready, 7)
            act.activation(tw[:], z[:, 0, 1:L + 1], ACT.Tanh).then_inc(pre_act, 1)
            act.activation(sgd[:], z[:, 2:4, 1:L + 1], ACT.Sigmoid).then_inc(pre_act, 1)
            for f in range(RT):
                act.wait_ge(pre_pe, 1)
                act.activation(sw[:, f], ps[:, f, 0:L], ACT.Sigmoid, bias=vcol("w0", f)).then_inc(pre_act, 1)
            for f in range(RT):
                act.wait_ge(pre_pe, 2)
                act.activation(b_[:, f], ps[:, f, 0:L], ACT.Sigmoid, bias=vcol("a0", f)).then_inc(pre_act, 1)
            act.wait_ge(pre_pe, 3)
            act.activation(gate[:], ps[:, :, 0:L], ACT.Copy).then_inc(pre_act, 1)
            act.wait_ge(pre_dve, 1)
            act.activation(kksq[:], kn[:], ACT.Square).then_inc(pre_act, 1)
            act.wait_ge(pre_pe, 4)
            act.activation(kksq[:], ps[:, :, 0:L], ACT.Sqrt).then_inc(pre_act, 1)

            def decays(c):
                n, t0 = CHUNK_LENGTHS[c], T0[c]
                if c:
                    act.wait_ge(fac_ready, c)
                    act.wait_ge(bk_ready, 4 * c)
                act.activation(pe1[:, :, 1:n + 1], cum[:, :, t0:t0 + n], ACT.Exp, scale=-DECAY_SCALE).then_inc(exp_ready, 1)
                act.activation(pinv[:, :, 0:n], cum[:, :, t0:t0 + n], ACT.Exp, scale=DECAY_SCALE).then_inc(exp_ready, 1)
                if c:
                    act.wait_ge(v_done, nth(c - 1))
                if n < C:
                    act.wait_ge(zeroed, u_zero(c) + 3)
                act.activation(vd[:, :, :].rearrange("p f (e t) -> p f e t", e=2)[:, :, :, 0:n],
                               z[:, 20:28, 1 + t0:1 + t0 + n].unsqueeze(2).broadcast_to([P, RT, 2, n]),
                               ACT.Copy).then_inc(vd_ready, 1)

            act.wait_ge(pre_dve, 8)
            decays(0)
            for c in range(N_RC + 1):
                if c:
                    for half in range(2):
                        act.wait_ge(z_done, nth(c - 1, half))
                        act.activation(tiles(zb, half), bank(6 + half), ACT.Copy).then_inc(zb_ready, 1)
                    for half in range(2):
                        act.wait_ge(u_done, nth(c - 1, half))
                        for e in range(2):
                            act.activation(tiles(xuv[(c - 1) % 2], half)[HEAD_ROWS[e], :, 64 * e:64 * e + 64],
                                           bank(6 + half)[HEAD_ROWS[e], :, 64 * e:64 * e + 64],
                                           ACT.Copy).then_inc(x_ready, 1)
                if c < N_RC:
                    for half in range(2):
                        act.wait_ge(bk_turned, nth(c, half))
                        if c:
                            act.wait_ge(s_done, nth(c - 1))
                        act.activation(tiles(bkt, half), bank(4 + half), ACT.Copy).then_inc(bkt_ready, 1)
                if c:
                    n, t0 = CHUNK_LENGTHS[c - 1], T0[c - 1]
                    for half in range(2):
                        act.wait_ge(y_done, nth(c - 1, half))
                        for e in range(2):
                            act.activation(z[HEAD_ROWS[e], 4 + 4 * half:8 + 4 * half, 1 + t0:1 + t0 + n],
                                           bank(half)[HEAD_ROWS[e], :, 64 * e:64 * e + n], ACT.Copy).then_inc(y_ready, 1)
                if c == N_RC:
                    continue
                for half in range(2):
                    act.wait_ge(v_done, nth(c, half))
                    act.wait_ge(zeroed, u_zero(c))
                    for e in range(2):
                        rows = HEAD_ROWS[1 - e]
                        act.activation(tiles(xuv[c % 2], half)[rows, :, 64 * e:64 * e + 64],
                                       bank(4 + half)[rows, :, 64 * e:64 * e + 64], ACT.Copy).then_inc(v_ready, 1)
                for l in range(1, LEVELS[c]):
                    for half in range(2):
                        act.wait_ge(q_done, inner(c, l, half))
                        act.activation(tiles(qb, half), bank(half), ACT.Copy).then_inc(q_ready, 1)
                    if l == 1 and c + 1 < N_RC:
                        decays(c + 1)
            act.wait_ge(pre_dve, 9)
            act.activation(yc2[:], yc[:], ACT.Square).then_inc(pre_act, 1)
            act.wait_ge(pre_dve, 10)
            act.activation(yc2[:], yc2[:], ACT.Sqrt).then_inc(pre_act, 1)
            act.wait_ge(pre_dve, 11)
            act.activation(yrh[:], yc[:], ACT.Copy).then_inc(y_high, 1)
            act.dma_start(h[:], d["ht"]).then_inc(h_landed, 16)

            plain("w_out", lambda g: mix_group("w_out", g, mix, LG))
            take_root(SUM["w_out"], LG)

            def residual_tile(name, k, t0, gain, base):
                act.wait_ge(h_ready, base + k + 1)
                x_tile(name, k, t0, gain)

            def feed_forward(name, block2):
                first = FIRST[name]
                P0 = PAIRS if block2 else 0

                def gated(p):
                    if not (isinstance(p, int) and p + P0 == 0):
                        act.wait_ge(av_ready, p + P0)
                    act.wait_ge(cv_ready, p + P0 + 1)
                    act.activation(sg[:], cv[:], ACT.Silu).then_inc(sg_ready, 1)

                def activated(p):
                    act.wait_ge(av_ready, p + P0 + 1)
                    act.activation(acth[:, bass.ds(p * 4, 4), :], av[:], ACT.Copy).then_inc(act_high, 1)

                def pair(p):
                    highs(p * 16 + (first + 12), 3)
                    gated(p)
                    highs(p * 16 + (first + 15), 9, 3)
                    activated(p)
                    highs(p * 16 + (first + 24), 4)

                pair(0)
                with act.Fori(1, PAIRS - 1) as p:
                    pair(p)
                last = first + 16 * PAIRS - 4
                highs(last, 3)
                gated(PAIRS - 1)
                highs(last + 3, 5, 3)
                activated(PAIRS - 1)

            opening("gate_up", lambda k: residual_tile("gate_up", k, TG, "g_pre_ffn", 0))
            feed_forward("gate_up", False)
            plain("down", lambda g: mix_group("down", g, mixf, SEQ))
            take_root(SUM["down"], SEQ)

            opening("in2", lambda k: residual_tile("in2", k, TU, "norm0", 16))
            act.dma_start(sinks[:], d["sinks"]).then_inc(sinks_landed, 16)
            act.wait_ge(bias_stored, 16)
            act.wait_ge(x_high, 48)
            bias_src = bass.AP(scratch.tensor, 0, [[1, P], [384, N_HEADS], [1, SEQ]])
            act.dma_start(bias[:], bias_src).then_inc(bias_landed, 16)
            plain("in2", lambda g: None, skip_first=True)

            def softmax_head(i):
                s = i % SLOTS
                act.wait_ge(max_ready, i + 1)
                if i >= SLOTS:
                    act.wait_ge(p_turned, i - SLOTS + 1)
                act.activation(pr[:, s, 0:QB], sc[:, s, 0:QB], ACT.Exp, bias=negmax[:, s, 0:1],
                               accum_out=rowsum[:, s, 0:1])
                act.activation(pr[:, s, QB:384], sc[:, s, QB:384], ACT.Exp, bias=negmax[:, s, 1:2],
                               accum_out=rowsum[:, s, 1:2])
                act.activation(esink[:, s, :], negmax[:, s, :], ACT.Exp, bias=sinks[:, head(i):head(i) + 1]).then_inc(p_ready, 1)

            def turn_out(i):
                grp, j = divmod(i, 4)
                act.wait_ge(p_turned, i + 1)
                if grp >= 2:
                    act.wait_ge(o_done, grp - 1)
                act.activation(pt[:, grp % 2, :, j, :], ps[:, 2 + i % 2, 0:384].rearrange("p (c q) -> p c q", c=3),
                               ACT.Copy).then_inc(pt_ready, 1)

            def out_high(grp):
                g2, e = divmod(grp, 2)
                act.wait_ge(o_done, grp + 1)
                rows = slice(64 * e, 64 * e + 64)
                for b in range(2):
                    act.activation(y2h[rows, 4 * g2:4 * g2 + 4, b * QB:(b + 1) * QB],
                                   ps[rows, 4 + 2 * (grp % 2) + b, :].rearrange("p (j q) -> p j q", j=4),
                                   ACT.Copy).then_inc(o_high, 1)

            def head(i):
                g2, e, j = i // 8, i // 4 % 2, i % 4
                return 4 * (2 * g2 + e) + j

            act.wait_ge(sinks_landed, 16)
            act.wait_ge(v_turned, 1)
            act.activation(vt[:], ps[:, 0:2, :], ACT.Copy).then_inc(vt_ready, 1)
            for i in range(N_HEADS + 6):
                if i < N_HEADS:
                    softmax_head(i)
                if 4 <= i < N_HEADS + 4:
                    turn_out(i - 4)
                if i >= 9 and (i - 9) % 4 == 0:
                    out_high((i - 9) // 4)
            plain("out2", lambda g: mix_group("out2", g, mix2, SEQ))
            take_root(SUM["out2"], SEQ)
            opening("up2", lambda k: residual_tile("up2", k, TU, "norm2", 32))
            feed_forward("up2", True)
            plain("down2", lambda g: mix_group("down2", g, mixf, SEQ))
            take_root(SUM["down2"], SEQ)

        @block.vector
        def _(dve):
            steps = Count()

            def low(n, slot):
                dve.wait_ge(high_ready, n + 1)
                dve.tensor_tensor(wl[:, slot], raw[:, slot], wh[:, slot].bitcast(F32), ALU.subtract).then_inc(low_ready, 1)

            def lows(first, count, slot=0):
                for c in range(count):
                    low(first + c, (slot + c) % RING)

            def clamp(first, count):
                return max(0, min(count, N_CHUNKS - first))

            def more(first, count):
                slot = first % RING
                with dve.Fori(0, count // RING) as i:
                    lows(i * RING + first, RING, slot)
                lows(first + count // RING * RING, count % RING, slot)

            def mean_of(s, bank, n, dst):
                dve.wait_ge(ss_done, s + 1)
                dve.tensor_scalar(mean_sq[:, 0:n], ps[:, bank, 0:n], 1.0 / D, RMS_EPS, ALU.mult, ALU.add).then_inc(ms_ready, 1)
                dve.wait_ge(root_ready, s + 1)
                dve.reciprocal(dst[:, 0:n], root[:, 0:n]).then_inc(rstd_ready, 1)
                dve.wait_ge(rstd_ready, s + 1)

            def x_low_tile(name, k, t0, gain):
                n = TOKENS[name]
                dve.wait_ge(x_high, 16 * XSPLIT[name] + k + 1)
                dve.scalar_tensor_tensor(xl[:, k, 0:n], h[:, k, t0:t0 + n], vcol(gain, k), xh[:, k, 0:n].bitcast(F32),
                                         ALU.mult, ALU.subtract).then_inc(x_low, 1)

            def opening(name, tile, finish):
                first = FIRST[name]
                for c in range(8):
                    tile(2 * c)
                    tile(2 * c + 1)
                    if c == 7:
                        finish()
                    if c >= 3:
                        lows(first + 4 + c - 3, 1, (c - 3) % RING)
                lows(first + 9, 3, 1)
                mean_of(SUM[name], 4, TOKENS[name], rstd)

            def plain(name, evacuate, skip_first=False):
                first, per = FIRST[name], CHUNKS[name]
                for g in range(1 if skip_first else 0, GROUPS[name]):
                    start = first + g * per + RING
                    count = clamp(start, per)
                    head = min(count, 1)
                    lows(start, head, start % RING)
                    if g:
                        evacuate(g - 1)
                    if count - head > 8:
                        more(start + head, count - head)
                    else:
                        lows(start + head, count - head, (start + head) % RING)
                evacuate(GROUPS[name] - 1)

            def group_full(name, g):
                ahead = 4 if (name, g) == ("w_out", 0) else 0
                dve.wait_ge(chunk_used, FIRST[name] + (g + 1) * CHUNKS[name] + ahead)

            def banks(g, t, n):
                b = 4 * (g % 2)
                return ps[:, b:b + 4, t:t + n]

            dve.wait_ge(vec_landed, 16)
            dve.wait_ge(h_landed, 16 * 4)
            lows(0, 4)
            opening("w_in", lambda k: x_low_tile("w_in", k, 0, "g_pre_mix"), lambda: None)

            def evacuate_in(g):
                group_full("w_in", g)
                b = 4 * (g % 2)
                if g < 7:
                    if g == 0:
                        dve.wait_ge(z_edge_zero, 1)
                    dve.tensor_tensor(z[:, 4 * g:4 * g + 4, 1:L + 1], ps[:, b:b + 4, 0:L], over(rstd[:, 0:L], 4),
                                      ALU.mult).then_inc(group_read, 1)
                    dve.wait_ge(group_read, g + 1)
                    dve.tensor_tensor(zd[:], z[:, 4 * g:4 * g + 4, 0:L], z[:, 4 * g:4 * g + 4, 1:L + 1],
                                      ALU.subtract).then_inc(dve_step, 1)
                    t = steps.add()
                    dve.wait_ge(dve_step, t)
                    for k in range(4 * g, 4 * g + 4):
                        last = dve.scalar_tensor_tensor(z[:, k, 1:L + 1], zd[:, k % 4], vcol("mu", k), z[:, k, 1:L + 1],
                                                        ALU.mult, ALU.add)
                    last.then_inc(z_ready, 1)
                    return
                half, part = divmod(g - 7, 3)
                if part == 0:
                    dve.tensor_tensor(cg[:], ps[:, b:b + 4, 0:LG + 2], over(rstd[:, TG - 2:L], 4),
                                      ALU.mult).then_inc(group_read, 1)
                elif part == 1:
                    dve.tensor_tensor(hg[:], ps[:, b:b + 4, 0:LG + 2], over(rstd[:, TG - 2:L], 4),
                                      ALU.mult).then_inc(group_read, 1)
                    dve.wait_ge(group_read, g + 1)
                    dve.tensor_tensor(cg[:], cg[:], hg[:], ALU.mult).then_inc(dve_step, 1)
                    t = steps.add()
                    dve.wait_ge(dve_step, t)
                    t = [0] * 4
                    for j in range(4):
                        dve.tensor_scalar(cc[:, j], cg[:, j, 0:LG], vcol("conv_w", 4 * half + j), None, ALU.mult).then_inc(dve_step, 1)
                        t[j] = steps.add()
                    for tap in (1, 2):
                        for j in range(4):
                            dve.wait_ge(dve_step, t[j])
                            dve.scalar_tensor_tensor(
                                cc[:, j], cg[:, j, tap:tap + LG], vcol("conv_w", RT * tap + 4 * half + j), cc[:, j],
                                ALU.mult, ALU.add).then_inc(dve_step, 1)
                            t[j] = steps.add()
                else:
                    dve.wait_ge(dve_step, steps.n)
                    if half:
                        dve.wait_ge(y_high, half)
                    dve.tensor_tensor(bg[:], ps[:, b:b + 4, 2:LG + 2], over(rstd[:, TG:L], 4), ALU.mult).then_inc(group_read, 1)
                    dve.wait_ge(group_read, g + 1)
                    dve.tensor_tensor(bg[:], bg[:], cc[:], ALU.mult).then_inc(yv_ready, 1)
                    dve.wait_ge(yv_ready, half + 1)
                    dve.wait_ge(y_high, half + 1)
                    dve.tensor_tensor(ycl[:, 4 * half:4 * half + 4], bg[:], ych[:, 4 * half:4 * half + 4].bitcast(F32),
                                      ALU.subtract).then_inc(y_low, 1)

            plain("w_in", evacuate_in, skip_first=True)

            dve.wait_ge(consts, 16 * 6)
            dve.wait_ge(bias_mm, 1)
            dve.tensor_tensor(erow[:], ps[0:32, 7, 0:384], maskrow[:], ALU.add).then_inc(erow_ready, 1)

            dve.wait_ge(dve_step, steps.n)
            zk = z[:, 12:20, 1:L + 1]
            zr = z[:, 4:12, 1:L + 1]
            zv = z[:, 20:28, 1:L + 1]
            for f in range(RT):
                last = dve.tensor_scalar(kn[:, f], z[:, 12 + f, 1:L + 1], vcol("k_k", f), None, ALU.mult)
            last.then_inc(pre_dve, 1)
            dve.wait_ge(pre_act, 10)
            dve.wait_ge(lora_landed, 16 * 6)
            dve.wait_ge(bias_stored, 16)
            for f in range(RT):
                last = dve.tensor_tensor_scan(cum[:, f], reset[:], sw[:, f], 0.0, ALU.mult, ALU.add)
            last.then_inc(pre_dve, 1)
            dve.wait_ge(pre_act, 18)
            for f in range(RT):
                dve.tensor_scalar(rkr[:, f], b_[:, f], -1.0, vcol("k_a", f), ALU.add, ALU.mult).then_inc(dve_step, 1)
                steps.add()
            dve.wait_ge(dve_step, steps.n)
            dve.scalar_tensor_tensor(zk, rkr[:], 1.0, zk, ALU.add, ALU.mult).then_inc(dve_step, 1)
            steps.add()
            dve.wait_ge(dve_step, steps.n)
            for f in range(RT):
                last = dve.scalar_tensor_tensor(rkr[:, f], z[:, 4 + f, 1:L + 1], vcol("r_k", f), z[:, 12 + f, 1:L + 1],
                                                ALU.mult, ALU.mult)
            last.then_inc(pre_dve, 1)
            dve.wait_ge(pre_act, 21)
            dve.tensor_scalar(kksq[:], kksq[:], 1e-12, None, ALU.max).then_inc(dve_step, 1)
            steps.add()
            dve.wait_ge(dve_step, steps.n)
            dve.reciprocal(kksq[:], kksq[:]).then_inc(dve_step, 1)
            steps.add()
            dve.wait_ge(dve_step, steps.n)
            dve.scalar_tensor_tensor(kn[:], kn[:], -1.0, kksq[:], ALU.mult, ALU.mult).then_inc(pre_dve, 1)
            dve.wait_ge(pre_dve, 4)
            dve.scalar_tensor_tensor(b_[:], kn[:], -1.0, b_[:], ALU.mult, ALU.mult).then_inc(pre_dve, 1)
            dve.wait_ge(pre_pe, 5)
            dve.tensor_tensor(bonus[:], ps[:, :, 0:L], zv, ALU.mult).then_inc(pre_dve, 1)
            dve.memset(pe1[:, :, 0:1], 1.0).then_inc(pre_dve, 1)
            dve.memset(st[:], 0.0).then_inc(pre_dve, 1)
            dve.wait_ge(pre_dve, 8)

            def factors(c, part, half):
                n, t0 = CHUNK_LENGTHS[c], T0[c]
                if part == 0 and half == 0:
                    dve.wait_ge(exp_ready, 2 * c + 2)
                    if c >= 2:
                        dve.wait_ge(y_done, nth(c - 2))
                    if n < C:
                        dve.wait_ge(zeroed, u_zero(c) + 1)
                    dve.tensor_copy(pend[:, c], pe1[:, :, n])
                src = kn[:, :, t0:t0 + n] if part == 0 else z[:, 4:12, 1 + t0:1 + t0 + n]
                decay = pe1[:, :, 0:n] if part == 0 else pe1[:, :, 1:n + 1]
                last = dve.tensor_tensor(
                    tiles(ar[c % 2], half).rearrange("p f (e t) -> p f e t", e=4)[:, :, 2 * part:2 * part + 2, 0:n],
                    tiles(src, half).unsqueeze(2).broadcast_to([P, HALF_TILES, 2, n]),
                    tiles(decay, half).unsqueeze(2).broadcast_to([P, HALF_TILES, 2, n]), ALU.mult)
                if part and half:
                    last.then_inc(fac_ready, 1)

            def level_matrix(c, l, half):
                if l >= 3:
                    dve.wait_ge(q_done, inner(c, l - 2, half))
                elif l == 2:
                    dve.wait_ge(am_turned, nth(c, half))
                dve.tensor_tensor(tiles(am[l % 2], half), tiles(ga, half), over(lmask[:, l], HALF_TILES),
                                  ALU.mult).then_inc(am_ready, 1)

            for part in range(2):
                for half in range(2):
                    factors(0, part, half)
            for c in range(N_RC + 1):
                if c < N_RC:
                    if c:
                        dve.wait_ge(z_done, nth(c - 1))
                    for half in range(2):
                        dve.wait_ge(gram_done, nth(c, half))
                        for part, dst in ((0, ga), (1, gr[c % 2])):
                            for e in range(2):
                                dve.tensor_tensor(tiles(dst, half)[:, :, 64 * e:64 * e + 64],
                                                  bank(2 * e + half)[:, :, 64 * part:64 * part + 64],
                                                  over(gmask[:, part], HALF_TILES), ALU.mult).then_inc(dve_step, 1)
                                steps.add()
                        dve.wait_ge(dve_step, steps.n)
                        level_matrix(c, 0, half)
                    for half in range(2):
                        dve.wait_ge(am_ready, level(c, 0, half))
                        if c:
                            dve.wait_ge(u_done, nth(c - 1, half))
                        dve.tensor_tensor(tiles(tt, half), tiles(am[0], half), over(ident[:], HALF_TILES),
                                          ALU.add).then_inc(dve_step, 1)
                        steps.add()
                        level_matrix(c, 1, half)
                if c and c < N_RC:
                    for half in range(2):
                        dve.wait_ge(s_done, nth(c - 1, half))
                        dve.wait_ge(y_done, nth(c - 1, half))
                        if c > 1:
                            dve.wait_ge(st_ready, nth(c - 2))
                        for e in range(2):
                            rows, cols = HEAD_ROWS[e], slice(64 * e, 64 * e + 64)
                            dve.tensor_tensor(tiles(st, half)[rows, :, cols], tiles(st, half)[rows, :, cols],
                                              bank(6 + half)[rows, :, cols], ALU.add).then_inc(dve_step, 1)
                            steps.add()
                        dve.wait_ge(dve_step, steps.n)
                        dve.tensor_tensor(tiles(st, half), tiles(st, half),
                                          tiles(pend[:, c - 1], half).unsqueeze(2).broadcast_to([P, HALF_TILES, P]),
                                          ALU.mult).then_inc(st_ready, 1)
                if c == N_RC:
                    continue
                for half in range(2):
                    dve.wait_ge(am_turned, nth(c, half))
                    dve.wait_ge(dve_step, steps.n)
                    dve.tensor_tensor(tiles(tn, half), bank(2 + half), over(ident[:], HALF_TILES), ALU.add).then_inc(tt_ready, 1)
                for l in range(1, LEVELS[c]):
                    for half in range(2):
                        if l + 1 < LEVELS[c]:
                            level_matrix(c, l + 1, half)
                        dve.wait_ge(tt_ready, level(c, l - 1, half))
                        dve.wait_ge(d_done, inner(c, l, half))
                        if l < LEVELS[c] - 1:
                            dve.tensor_tensor(tiles(tn, half), tiles(tn, half), bank(2 + half), ALU.add)
                        dve.tensor_tensor(tiles(tt, half), tiles(tt, half), bank(4 + half), ALU.add).then_inc(tt_ready, 1)
                    if l <= 4 and c + 1 < N_RC:
                        factors(c + 1, *divmod(l - 1, 2))
            dve.wait_ge(pre_pe, 6)
            zy = z[:, 4:12, 1 + TG:1 + L]
            dve.scalar_tensor_tensor(yc[:], ps[:, :, 0:LG], -1.0 / HEAD, zy, ALU.mult, ALU.add).then_inc(pre_dve, 1)
            dve.wait_ge(pre_dve, 9)
            dve.wait_ge(pre_pe, 7)
            dve.tensor_scalar(yc2[:], ps[:, :, 0:LG], 1.0 / HEAD, GN_EPS, ALU.mult, ALU.add).then_inc(pre_dve, 1)
            dve.wait_ge(pre_act, 23)
            dve.reciprocal(yc2[:], yc2[:]).then_inc(dve_step, 1)
            steps.add()
            dve.wait_ge(dve_step, steps.n)
            dve.tensor_tensor(yc[:], yc[:], yc2[:], ALU.mult).then_inc(dve_step, 1)
            steps.add()
            dve.wait_ge(dve_step, steps.n)
            for f in range(RT):
                dve.tensor_scalar(yc[:, f], yc[:, f], vcol("ln_w", f), vcol("ln_b", f), ALU.mult, ALU.add).then_inc(dve_step, 1)
                steps.add()
            dve.wait_ge(dve_step, steps.n)
            dve.tensor_tensor(yc[:], yc[:], bonus[:, :, TG:L], ALU.add).then_inc(dve_step, 1)
            steps.add()
            dve.wait_ge(dve_step, steps.n)
            dve.tensor_tensor(yc[:], yc[:], gate[:, :, TG:L], ALU.mult).then_inc(pre_dve, 1)
            dve.wait_ge(pre_dve, 11)
            dve.wait_ge(y_high, 3)
            dve.tensor_tensor(yrl[:], yc[:], yrh[:].bitcast(F32), ALU.subtract).then_inc(y_low, 1)

            def mix_out(name, dst, n):
                def evacuate(g):
                    group_full(name, g)
                    dve.tensor_copy(dst[:, 4 * g:4 * g + 4, :], banks(g, 0, n)).then_inc(group_read, 1)
                return evacuate

            plain("w_out", mix_out("w_out", mix, LG))
            mean_of(SUM["w_out"], 0, LG, rstd_post)
            dve.wait_ge(group_read, G0["gate_up"])
            dve.wait_ge(h_landed, 16 * 5)

            def residual_tile(name, src, n, t0, post_gain, base):
                def tile(k):
                    dve.tensor_tensor(scaled[:, k % 2, 0:n], src[:, k, 0:n], rstd_post[:, 0:n], ALU.mult).then_inc(dve_step, 1)
                    t = steps.add()
                    dve.wait_ge(dve_step, t)
                    dve.scalar_tensor_tensor(h[:, k, t0:t0 + n], scaled[:, k % 2, 0:n], vcol(post_gain, k),
                                             h[:, k, t0:t0 + n], ALU.mult, ALU.add).then_inc(h_ready, 1)
                    if name and k:
                        dve.wait_ge(h_ready, base + k)
                        x_low_tile(name, k - 1, t0, {"gate_up": "g_pre_ffn", "in2": "norm0", "up2": "norm2"}[name])
                return tile

            def last_low(name, t0, gain, base):
                def finish():
                    dve.wait_ge(h_ready, base + KT)
                    x_low_tile(name, KT - 1, t0, gain)
                return finish

            def convolve(dst, tile0, taps, stride, between, done=None):
                t = [0] * 4
                for j in range(4):
                    dve.tensor_scalar(dst[:, j], gt[:, j, 0:SEQ], vcol(taps, tile0 + j), None, ALU.mult).then_inc(dve_step, 1)
                    t[j] = steps.add()
                between(0)
                for tap in (1, 2):
                    if tap == 2:
                        between(1)
                    for j in range(4):
                        dve.wait_ge(dve_step, t[j])
                        ins = dve.scalar_tensor_tensor(dst[:, j], gt[:, j, tap:tap + SEQ],
                                                       vcol(taps, tile0 + (stride * tap + j)), dst[:, j],
                                                       ALU.mult, ALU.add)
                        if done is not None and tap == 2 and j == 3:
                            ins.then_inc(done, 1)
                        else:
                            ins.then_inc(dve_step, 1)
                            t[j] = steps.add()

            def feed_forward(name, block2):
                first = FIRST[name]
                P0 = PAIRS if block2 else 0
                n = TOKENS[name]

                def gated(p):
                    def between(x):
                        lows(p * 16 + (first + 13 + x), 1, 1 + x)

                    dve.wait_ge(chunk_used, p * 16 + (first + 8))
                    if not (isinstance(p, int) and p + P0 == 0):
                        dve.wait_ge(sg_ready, p + P0)
                    off = 2 if block2 else 0
                    dve.tensor_tensor(gt[:, :, off:off + n], ps[:, 0:4, 0:n], over(rstd[:, 0:n], 4), ALU.mult).then_inc(group_read, 1)
                    dve.wait_ge(group_read, p * 2 + (G0[name] + 1))
                    convolve(cv, p * 4, "conv_ffn2" if block2 else "conv_ffn", 2 * FT if block2 else FT, between,
                             cv_ready)

                def upped(p):
                    def between(x):
                        if not isinstance(p, int) or p < PAIRS - 1:
                            lows(p * 16 + (first + 21 + x), 1, 1 + x)

                    dve.wait_ge(chunk_used, p * 16 + (first + 16))
                    if block2:
                        dve.tensor_tensor(gt[:, :, 2:2 + SEQ], ps[:, 4:8, 0:SEQ], over(rstd[:, 0:SEQ], 4),
                                          ALU.mult).then_inc(group_read, 1)
                        dve.wait_ge(group_read, p * 2 + (G0[name] + 2))
                        convolve(ut, p * 4 + FT, "conv_ffn2", 2 * FT, between)
                        dve.wait_ge(dve_step, steps.n)
                    else:
                        dve.tensor_tensor(ut[:], ps[:, 4:8, 0:SEQ], over(rstd[:, 2:2 + SEQ], 4), ALU.mult).then_inc(group_read, 1)
                        dve.wait_ge(group_read, p * 2 + (G0[name] + 2))
                        between(0)
                        between(1)
                    dve.wait_ge(sg_ready, p + P0 + 1)
                    dve.tensor_tensor(av[:], sg[:], ut[:], ALU.mult).then_inc(av_ready, 1)

                def split(p):
                    dve.wait_ge(av_ready, p + P0 + 1)
                    dve.wait_ge(act_high, p + P0 + 1)
                    dve.tensor_tensor(actl[:, bass.ds(p * 4, 4), :], av[:], acth[:, bass.ds(p * 4, 4), :].bitcast(F32),
                                      ALU.subtract).then_inc(act_low, 1)

                per_turn = 11 + (12 if block2 else 0)
                def pair(p):
                    lows(p * 16 + (first + 12), 1)
                    gated(p)
                    lows(p * 16 + (first + 15), 6, 3)
                    upped(p)
                    lows(p * 16 + (first + 23), 1, 3)
                    split(p)
                    lows(p * 16 + (first + 24), 4)

                pair(0)
                with dve.Fori(1, PAIRS - 1) as p:
                    steps.enter(p, 1, per_turn)
                    pair(p)
                    steps.leave(PAIRS - 2)
                last = first + 16 * PAIRS - 4
                lows(last, 1)
                gated(PAIRS - 1)
                lows(last + 3, 5, 3)
                upped(PAIRS - 1)
                split(PAIRS - 1)

            opening("gate_up", residual_tile("gate_up", mix, LG, TG, "g_post_mix", 0),
                    last_low("gate_up", TG, "g_pre_ffn", 0))
            feed_forward("gate_up", False)
            plain("down", mix_out("down", mixf, SEQ))
            mean_of(SUM["down"], 0, SEQ, rstd_post)
            dve.wait_ge(group_read, G0["in2"])

            opening("in2", residual_tile("in2", mixf, SEQ, TU, "g_post_ffn", 16), last_low("in2", TU, "norm0", 16))

            def evacuate_in2(g):
                group_full("in2", g)
                r = over(rstd[:, 0:SEQ], 4)
                if g < 4:
                    ins = dve.scalar_tensor_tensor(qf[:, 4 * g:4 * g + 4, :], banks(g, 0, SEQ), HEAD ** -0.5, r,
                                                   ALU.mult, ALU.mult)
                else:
                    ins = dve.tensor_tensor((kf if g == 4 else vf)[:], banks(g, 0, SEQ), r, ALU.mult)
                ins.then_inc(group_read, 1)

            plain("in2", evacuate_in2, skip_first=True)
            dve.wait_ge(bias_landed, 16)
            dve.wait_ge(sinks_landed, 16)

            def head(i):
                g2, e, j = i // 8, i // 4 % 2, i % 4
                return 4 * (2 * g2 + e) + j

            def scores(i):
                s = i % SLOTS
                dve.wait_ge(s_ready, i + 1)
                if i >= SLOTS:
                    dve.wait_ge(p_ready, i - SLOTS + 1)
                rev = bias[:, head(i), ::-1]
                dve.tensor_tensor_reduce(sc[:, s, 0:QB], ps[:, i % 2, 0:QB], rev[:, QB:SEQ], 1.0, MASKED, ALU.add, ALU.max,
                                         rowmax[:, s, 0:1])
                dve.tensor_tensor_reduce(sc[:, s, QB:384], ps[:, i % 2, QB:384], rev, 1.0, MASKED, ALU.add, ALU.max,
                                         rowmax[:, s, 1:2]).then_inc(sc_ready, 1)
                dve.wait_ge(sc_ready, i + 1)
                dve.tensor_scalar(negmax[:, s], rowmax[:, s], sinks[:, head(i):head(i) + 1], -1.0, ALU.max,
                                  ALU.mult).then_inc(max_ready, 1)

            def normalise(i):
                s = i % SLOTS
                dve.wait_ge(p_ready, i + 1)
                dve.tensor_tensor(denom[:, s], rowsum[:, s], esink[:, s], ALU.add).then_inc(dve_step, 1)
                t = steps.add()
                dve.wait_ge(dve_step, t)
                dve.reciprocal(rdenom[:, s], denom[:, s]).then_inc(dve_step, 1)
                t = steps.add()
                dve.wait_ge(dve_step, t)
                dve.tensor_scalar(pr[:, s, 0:QB], pr[:, s, 0:QB], rdenom[:, s, 0:1], None, ALU.mult)
                dve.tensor_scalar(pr[:, s, QB:384], pr[:, s, QB:384], rdenom[:, s, 1:2], None, ALU.mult).then_inc(pn_ready, 1)

            def out_low(grp):
                g2, e = divmod(grp, 2)
                dve.wait_ge(o_high, 2 * grp + 2)
                rows = slice(64 * e, 64 * e + 64)
                for b in range(2):
                    dst = (slice(64 * e, 64 * e + 64), slice(4 * g2, 4 * g2 + 4), slice(b * QB, (b + 1) * QB))
                    dve.tensor_tensor(y2l[dst], ps[rows, 4 + 2 * (grp % 2) + b, :].rearrange("p (j q) -> p j q", j=4),
                                      y2h[dst].bitcast(F32), ALU.subtract).then_inc(o_low, 1)

            for i in range(N_HEADS + 6):
                if i < N_HEADS:
                    scores(i)
                if 2 <= i < N_HEADS + 2:
                    normalise(i - 2)
                if i >= 9 and (i - 9) % 4 == 0:
                    out_low((i - 9) // 4)
            plain("out2", mix_out("out2", mix2, SEQ))
            mean_of(SUM["out2"], 0, SEQ, rstd_post)
            dve.wait_ge(group_read, G0["up2"])
            opening("up2", residual_tile("up2", mix2, SEQ, TU, "norm1", 32), last_low("up2", TU, "norm2", 32))
            dve.memset(gt[:, :, 0:2], 0.0)
            feed_forward("up2", True)
            plain("down2", mix_out("down2", mixf, SEQ))
            mean_of(SUM["down2"], 0, SEQ, rstd_post)
            dve.wait_ge(group_read, G0["down2"] + 4)
            tile = residual_tile(None, mixf, SEQ, TU, "norm3", 48)
            for k in range(KT):
                tile(k)

        @block.tensor
        def _(pe):

            def group(name, g, parity, moving, n, before=None):
                per = CHUNKS[name]
                chunks_of(name, g * per + FIRST[name], (FIRST[name] + parity * per) % RING, parity, moving, n,
                          range(per), before)

            def chunks_of(name, n0, slot0, parity, moving, n, rows, before=None):
                per = CHUNKS[name]
                for c in rows:
                    pe.wait_ge(low_ready, n0 + (c - rows[0] + 1))
                    slot = (slot0 + c - rows[0]) % RING
                    for kk in range(2):
                        k = 2 * c + kk
                        if before:
                            before(k)
                        hi, lo = moving(k)
                        for m in range(4):
                            out = ps[:, 4 * parity + m, 0:n]
                            w_high, w_low = wh[:, slot, kk, m * P:(m + 1) * P], wl[:, slot, kk, m * P:(m + 1) * P]
                            pe.matmul(out, w_high, hi, start=(k == 0), stop=False)
                            pe.matmul(out, w_high, lo, start=False, stop=False)
                            last = pe.matmul(out, w_low, hi, start=False, stop=(k == 2 * per - 1))
                    last.then_inc(chunk_used, 1)

            def square_sum(name, bank):
                s = SUM[name]
                n = TOKENS[name]
                pe.wait_ge(sq_added, 16 * (s + 1))
                pe.matmul(ps[:, bank, 0:n], ones[:], sq_sum[:, 0:n], start=True, stop=True).then_inc(ss_done, 1)

            def whole(name, moving, n, before):
                for parity in range(2):
                    pe.wait_ge(group_read, G0[name] + parity - 1)
                    group(name, parity, parity, moving, n, None if parity else before)
                with pe.Fori(1, GROUPS[name] // 2) as i:
                    for parity in range(2):
                        pe.wait_ge(group_read, 2 * i + (G0[name] + parity - 1))
                        group(name, 2 * i + parity, parity, moving, n)
                square_sum(name, 0)

            def x_of(n):
                return lambda k: (xh[:, k, 0:n], xl[:, k, 0:n])

            def tile_ready(name):
                return lambda k: pe.wait_ge(x_low, 16 * XSPLIT[name] + k + 1)

            group("w_in", 0, 0, x_of(L), L, tile_ready("w_in"))
            pe.wait_ge(consts, 16 * 6)
            square_sum("w_in", 4)
            pe.wait_ge(ms_ready, 1)
            group("w_in", 1, 1, x_of(L), L)
            with pe.Fori(1, 3) as i:
                for parity in range(2):
                    pe.wait_ge(group_read, 2 * i + (parity - 1))
                    group("w_in", 2 * i + parity, parity, x_of(L), L)
            pe.wait_ge(group_read, 5)
            group("w_in", 6, 0, x_of(L), L)

            def x_conv(k):
                return xh[:, k, TG - 2:L], xl[:, k, TG - 2:L]

            with pe.Fori(3, 6) as i:
                for parity in (1, 0):
                    pe.wait_ge(group_read, 2 * i + (1 - parity))
                    group("w_in", 2 * i + (2 - parity), parity, x_conv, L - TG + 2)

            pe.wait_ge(group_read, 13)
            pe.matmul(ps[0:32, 7, 0:384], table[:], onehot[:], start=True, stop=True).then_inc(bias_mm, 1)
            pe.wait_ge(erow_ready, 1)
            pe.wait_ge(lora_landed, 16 * 6)

            def per_tile(rhs, lhs, n, parts=1):
                for f in range(RT):
                    for k in range(parts):
                        last = pe.matmul(ps[:, f, 0:n], lhs(f, k), rhs(f, k), start=(k == 0), stop=(k == parts - 1))
                last.then_inc(pre_pe, 1)

            pe.wait_ge(pre_act, 1)
            per_tile(lambda f, k: tw[0:LORA, :], lambda f, k: wdu[:, f * P:(f + 1) * P], L)
            pe.wait_ge(pre_act, 10)
            per_tile(lambda f, k: z[0:LORA, 1, 1:L + 1], lambda f, k: aup[:, f * P:(f + 1) * P], L)
            pe.wait_ge(pre_act, 18)
            per_tile(lambda f, k: sgd[:, k, :], lambda f, k: gup[:, k, f * P:(f + 1) * P], L, 2)
            pe.wait_ge(pre_act, 20)
            per_tile(lambda f, k: kksq[:, f, :], lambda f, k: bones[:], L)
            pe.wait_ge(pre_act, 21)
            pe.wait_ge(pre_dve, 3)
            per_tile(lambda f, k: rkr[:, f, :], lambda f, k: bones[:], L)
            pe.wait_ge(pre_dve, 8)

            def batch(b, half, lhs, rhs, done, first=True):
                for i in range(HALF_TILES):
                    f = HALF_TILES * half + i
                    last = pe.matmul(ps[:, b, P * i:P * (i + 1)], lhs(f), rhs(f), start=True, stop=True)
                last.then_inc(done, 1)

            def two_terms(b, half, terms, done):
                for i in range(HALF_TILES):
                    f = HALF_TILES * half + i
                    for x, (lhs, rhs) in enumerate(terms):
                        last = pe.matmul(ps[:, b, P * i:P * (i + 1)], lhs(f), rhs(f), start=(x == 0), stop=(x == len(terms) - 1))
                last.then_inc(done, 1)

            def join(c, l, half):
                pe.wait_ge(q_ready, inner(c, l, half))
                if l < LEVELS[c] - 1:
                    for i in range(HALF_TILES):
                        f = HALF_TILES * half + i
                        pe.matmul(ps[:, 2 + half, P * i:P * (i + 1)], tt[:, f, :], qb[:, f, :], start=True, stop=True)
                batch(4 + half, half, lambda f: qb[:, f, :], lambda f: tt[:, f, :], d_done)

            def product(c, l, half):
                pe.wait_ge(am_ready, level(c, l, half))
                pe.wait_ge(tt_ready, level(c, l - 1, half))
                batch(half, half, lambda f: am[l % 2][:, f, :], lambda f: tn[:, f, :], q_done)

            for c in range(N_RC + 1):
                p = c - 1
                xp, arp, grp = xuv[p % 2], ar[p % 2], gr[p % 2]
                if c < N_RC:
                    pe.wait_ge(fac_ready, c + 1)
                    pe.wait_ge(bk_ready, 4 * c + 4)
                    if c:
                        pe.wait_ge(tt_ready, level(p, LEVELS[p] - 1))
                    for half in range(2):
                        for i in range(HALF_TILES):
                            f = HALF_TILES * half + i
                            for e in range(2):
                                last = pe.matmul(ps[:, 2 * e + half, P * i:P * (i + 1)], bkf[HEAD_ROWS[e], f, :],
                                                 ar[c % 2][HEAD_ROWS[e], f, 64:192], start=True, stop=True)
                        last.then_inc(gram_done, 1)
                if c:
                    pe.wait_ge(v_ready, 4 * c)
                    for half in range(2):
                        if p:
                            pe.wait_ge(st_ready, nth(p - 1, half))
                        terms = [(lambda f: ga[:, f, :], lambda f: xp[:, f, :]),
                                 (lambda f: arp[:, f, 0:P], lambda f: st[:, f, :])]
                        two_terms(6 + half, half, terms if p else terms[:1], z_done)
                if c < N_RC:
                    for half in range(2):
                        for i in range(HALF_TILES):
                            last = pe.transpose(ps[:, 4 + half, P * i:P * (i + 1)], bkf[:, HALF_TILES * half + i, :], ident[:])
                        last.then_inc(bk_turned, 1)
                if c:
                    if c == N_RC:
                        pe.wait_ge(tt_ready, level(p, LEVELS[p] - 1))
                    for half in range(2):
                        pe.wait_ge(zb_ready, nth(p, half))
                        batch(6 + half, half, lambda f: tt[:, f, :], lambda f: zb[:, f, :], u_done)
                    for half in range(2):
                        pe.wait_ge(x_ready, 2 * nth(p, half))
                        if c < N_RC:
                            batch(6 + half, half, lambda f: bkt[:, f, :], lambda f: xp[:, f, :], s_done)
                    for half in range(2):
                        if c < N_RC:
                            pe.wait_ge(am_ready, level(c, 0, half))
                        terms = [(lambda f: xp[:, f, :], lambda f: grp[:, f, :]),
                                 (lambda f: st[:, f, :], lambda f: arp[:, f, P:2 * P])]
                        two_terms(half, half, terms if p else terms[:1], y_done)
                if c == N_RC:
                    continue
                pe.wait_ge(vd_ready, c + 1)
                for half in range(2):
                    pe.wait_ge(bkt_ready, nth(c, half))
                    for i in range(HALF_TILES):
                        last = pe.transpose(ps[:, 4 + half, P * i:P * (i + 1)], vd[:, HALF_TILES * half + i, :], ident[:])
                    last.then_inc(v_done, 1)
                for half in range(2):
                    pe.wait_ge(am_ready, level(c, 0, half))
                    batch(2 + half, half, lambda f: am[0][:, f, :], lambda f: ident[:], am_turned)
                if c:
                    pe.wait_ge(y_ready, 4 * c)
                pe.wait_ge(v_ready, 4 * c + 4)
                for l in range(1, LEVELS[c]):
                    product(c, l, 0)
                    if l > 1:
                        join(c, l - 1, 1)
                    join(c, l, 0)
                    product(c, l, 1)
                join(c, LEVELS[c] - 1, 1)
            pe.wait_ge(y_ready, 4 * N_RC)
            per_tile(lambda f, k: z[:, 4 + f, 1 + TG:1 + L], lambda f, k: bones[:], LG)
            pe.wait_ge(pre_act, 22)
            per_tile(lambda f, k: yc2[:, f, :], lambda f, k: bones[:], LG)

            def y_of(k):
                if k < RT:
                    return ych[:, k, :], ycl[:, k, :]
                return yrh[:, k - RT, :], yrl[:, k - RT, :]

            pe.wait_ge(y_low, 2)
            pe.wait_ge(pre_dve, 10)
            for g, c0 in ((0, 0), (1, 0), (0, 4), (1, 4)):
                if c0:
                    pe.wait_ge(y_low, 3)
                chunks_of("w_out", FIRST["w_out"] + 2 * c0 + 4 * g, 0, g, y_of, LG, range(c0, c0 + 4))
            with pe.Fori(1, 2) as i:
                for parity in range(2):
                    pe.wait_ge(group_read, 2 * i + (G0["w_out"] + parity - 1))
                    group("w_out", 2 * i + parity, parity, y_of, LG)
            square_sum("w_out", 0)

            def feed_forward(name):
                n = TOKENS[name]
                r0 = G0[name]

                def x_up(k):
                    return (xh[:, k, n - SEQ:n], xl[:, k, n - SEQ:n])

                group(name, 0, 0, x_of(n), n, tile_ready(name))
                square_sum(name, 4)
                pe.wait_ge(ms_ready, SUM[name] + 1)
                group(name, 1, 1, x_up, SEQ)
                with pe.Fori(1, PAIRS) as p:
                    pe.wait_ge(group_read, 2 * p + (r0 - 1))
                    group(name, 2 * p, 0, x_of(n), n)
                    pe.wait_ge(group_read, 2 * p + r0)
                    group(name, 2 * p + 1, 1, x_up, SEQ)

            def down(name, p0):
                whole(name, lambda k: (acth[:, k, :], actl[:, k, :]), SEQ,
                      lambda k: pe.wait_ge(act_low, p0 + k // 4 + 1))

            feed_forward("gate_up")
            down("down", 0)

            group("in2", 0, 0, x_of(SEQ), SEQ, tile_ready("in2"))
            square_sum("in2", 4)
            pe.wait_ge(ms_ready, SUM["in2"] + 1)
            group("in2", 1, 1, x_of(SEQ), SEQ)
            with pe.Fori(1, 3) as i:
                pe.wait_ge(group_read, 2 * i + (G0["in2"] - 1))
                group("in2", 2 * i, 0, x_of(SEQ), SEQ)
                pe.wait_ge(group_read, 2 * i + G0["in2"])
                group("in2", 2 * i + 1, 1, x_of(SEQ), SEQ)

            pe.wait_ge(group_read, G0["out2"])
            for kb in range(2):
                for g2 in range(4):
                    last = pe.transpose(ps[:, kb, P * g2:P * (g2 + 1)], vf[:, g2, QB * kb:QB * (kb + 1)], ident[:])
            last.then_inc(v_turned, 1)
            pe.wait_ge(vt_ready, 1)

            def scores(i):
                g2, e, j = i // 8, i // 4 % 2, i % 4
                rows = slice(64 * e, 64 * e + 64)
                if i >= 2:
                    pe.wait_ge(sc_ready, i - 1)
                pe.matmul(ps[:, i % 2, 0:QB], qf[rows, 4 * g2 + j, 0:QB], kf[rows, g2, 0:QB], start=True, stop=True)
                pe.matmul(ps[:, i % 2, QB:384], qf[rows, 4 * g2 + j, QB:SEQ], kf[rows, g2, 0:SEQ], start=True,
                          stop=True).then_inc(s_ready, 1)

            def turn(i):
                pe.wait_ge(pn_ready, i + 1)
                if i >= 2:
                    pe.wait_ge(pt_ready, i - 1)
                for t in range(3):
                    last = pe.transpose(ps[:, 2 + i % 2, QB * t:QB * (t + 1)], pr[:, i % SLOTS, QB * t:QB * (t + 1)], ident[:])
                last.then_inc(p_turned, 1)

            def values(grp):
                g2, e = divmod(grp, 2)
                rows = slice(64 * e, 64 * e + 64)
                pe.wait_ge(pt_ready, 4 * grp + 4)
                if grp >= 2:
                    pe.wait_ge(o_low, 2 * (grp - 1))
                bank = 4 + 2 * (grp % 2)
                v = [vt[:, kb, P * g2 + 64 * e:P * g2 + 64 * e + 64] for kb in range(2)]
                for b, terms in enumerate((((0, 0),), ((0, 1), (1, 2)))):
                    for x, (kb, t) in enumerate(terms):
                        last = pe.matmul(ps[rows, bank + b, :], v[kb], pt[:, grp % 2, t, :, :].rearrange("p j q -> p (j q)"),
                                         start=(x == 0), stop=(x == len(terms) - 1))
                last.then_inc(o_done, 1)

            for i in range(N_HEADS + 5):
                if i < N_HEADS:
                    scores(i)
                if 3 <= i < N_HEADS + 3:
                    turn(i - 3)
                if i >= 8 and (i - 8) % 4 == 0:
                    values((i - 8) // 4)

            pe.wait_ge(o_low, 16)
            whole("out2", lambda k: (y2h[:, k, :], y2l[:, k, :]), SEQ, None)
            feed_forward("up2")
            down("down2", PAIRS)



def _features(v):
    return np.asarray(v).reshape(-1, P).T


def _chunks(w):
    rows, cols = w.shape
    w = w.reshape(rows // 256, 2, P, cols // 512, 512)
    return np.ascontiguousarray(w.transpose(3, 0, 2, 1, 4)).reshape(-1, P, 2, 512)


def _pad(w, axis, n):
    widths = [(0, 0)] * w.ndim
    widths[axis] = (0, n)
    return np.pad(w, widths)


def _lora_parts(v, axis):
    a, b, c = np.split(v, [LORA, 2 * LORA], axis=axis)
    return [_pad(a, axis, P - LORA), _pad(b, axis, P - LORA), c]


def _constants():
    i = np.arange(P)
    same_head = (i[:, None] // C == i[None, :] // C).astype(np.float32)
    src, dst = i[:, None] % C, i[None, :] % C
    lmask = np.stack([same_head * (src // (2 * m) == dst // (2 * m)) * (src % (2 * m) < m) * (dst % (2 * m) >= m)
                      for m in (1, 2, 4, 8, 16, 32)], axis=1)
    t = np.arange(C)[None, :]
    gmask = np.stack([(i[:, None] % C) < t, (i[:, None] % C) <= t], axis=1)
    reset = np.ones((P, L))
    reset[:, 0:L:C] = 0.0
    dist = np.arange(384) - (QB - 1)
    ok = (dist >= 0) & (dist < QB)
    near = np.maximum(dist, 0)
    far = np.log(np.maximum(near, 1).astype(np.float32) / np.float32(16)) / np.float32(math.log(8.0))
    bucket = np.where(near < 16, near, np.minimum(16 + (far * 16).astype(np.int32), 31))
    onehot = (np.arange(32)[:, None] == bucket[None, :]) & ok[None, :]
    maskrow = np.broadcast_to(np.where(ok, 0.0, MASKED), (32, 384))
    return {"ident": np.eye(P), "ones": np.ones((P, P)), "bones": same_head, "lmask": lmask, "gmask": gmask,
            "reset": reset, "onehot": onehot, "maskrow": maskrow}


_OUT = (P, KT, SEQ)


def kernel(**inputs):
    import concourse.bacc as bacc
    from concourse.bass_utils import run_bass_kernel_spmd

    a = {k: np.asarray(v) for k, v in inputs.items()}
    hidden = np.concatenate([a["meta_tokens"], a["x"][0]], axis=0)
    conv, rwkv = a["w_in"][:, :3 * RW], a["w_in"][:, 3 * RW:]
    gate_b, gate_c, hx = np.split(conv, 3, axis=1)
    columns = _lora_parts(rwkv[:, 3 * RW:], 1) + [rwkv[:, :3 * RW]]
    for half in range(2):
        cut = slice(512 * half, 512 * half + 512)
        columns += [gate_c[:, cut], hx[:, cut], gate_b[:, cut]]
    gate, up = np.split(a["w_gate_up"], 2, axis=1)
    gate_up = np.stack([gate.reshape(D, -1, 512), up.reshape(D, -1, 512)], axis=2).reshape(D, -1)
    up2 = a["ffn_w_up_2"][0].reshape(D, 2, -1, 512).transpose(0, 2, 1, 3).reshape(D, -1)
    heads = a["swa_w_in_2"][0][:, :D].reshape(D, 4, 2, 4, HEAD).transpose(0, 1, 3, 2, 4).reshape(D, D)
    in2 = np.concatenate([heads, a["swa_w_in_2"][0][:, D:]], axis=1)
    out2 = a["swa_w_out_2"][0].reshape(4, 2, 4, HEAD, D).transpose(0, 2, 1, 3, 4).reshape(D, D)
    mu = np.concatenate(_lora_parts(a["mu_rwkv"][3 * RW:], 0) + [a["mu_rwkv"][:3 * RW]])
    vectors = [a["g_pre_mix"], a["g_post_mix"], a["g_pre_ffn"], a["g_post_ffn"], *a["norm_g_2"][0], mu, a["w0"], a["a0"],
               a["k_k"], a["k_a"], a["r_k"].reshape(-1), a["ln_x_w"], a["ln_x_b"], a["conv_w"].reshape(-1),
               a["conv_ffn"].reshape(-1), a["ffn_conv_2"][0].reshape(-1)]
    w_out = _chunks(a["w_out"])
    w_out = w_out[np.r_[0:4, 8:12, 4:8, 12:32]]
    arrays = {
        "ht": hidden.T.reshape(KT, P, L).transpose(1, 0, 2),
        "w_in": _chunks(np.concatenate(columns, axis=1)), "w_out": w_out, "gate_up": _chunks(gate_up),
        "down": _chunks(a["w_down"]), "in2": _chunks(in2), "out2": _chunks(out2), "up2": _chunks(up2),
        "down2": _chunks(a["ffn_w_down_2"][0]),
        "vec": np.concatenate([_features(v) for v in vectors], axis=1),
        "wdu": a["w_decay_up"], "aup": a["a_up"], "gup": a["g_up"].reshape(2, P, RW).transpose(1, 0, 2),
        "table": a["rel_bias_table_2"], "sinks": np.broadcast_to(a["swa_sinks_2"][0], (P, N_HEADS)),
        **{k: np.asarray(v, np.float32) for k, v in _constants().items()},
    }
    nc = bacc.Bacc("TRN2", target_bir_lowering=False, num_devices=1, dynamic_dma_scratch_size=1024)
    named, d = {}, {}
    for name, v in arrays.items():
        v = np.ascontiguousarray(v)
        named[f"in_{name}"] = v
        d[name] = nc.dram_tensor(f"in_{name}", v.shape, mybir.dt.from_np(v.dtype), kind="ExternalInput").ap()
    d["out"] = nc.dram_tensor("out_0", _OUT, F32, kind="ExternalOutput").ap()
    program(nc, d)
    out = run_bass_kernel_spmd(nc, [named], core_ids=[0]).results[0]["out_0"]
    return np.ascontiguousarray(out.transpose(1, 0, 2).reshape(D, SEQ).T)[None]
```

```python
import math
from contextlib import ExitStack

import numpy as np

import concourse.bass as bass
from concourse import mybir

F32 = mybir.dt.float32
F32R = mybir.dt.float32r
ALU = mybir.AluOpType
ACT = mybir.ActivationFunctionType

P = 128
D = 2048
KT = D // P
SEQ = 256
N_META = 16
L = SEQ + N_META
D_FF = 5632
FT = D_FF // P
RW = D // 2
RT = RW // P
HEAD = 64
LORA = 96
N_HEADS = 32
QB = 128
DECAY_SCALE = math.exp(-0.5)
RMS_EPS = 1e-6
GN_EPS = 64e-5
MASKED = -1e30

LG = SEQ + 2
TG = L - LG
TU = L - SEQ

PROJECTIONS = [("w_in", 13, 8), ("w_out", 4, 8), ("gate_up", 22, 8), ("down", 4, 22),
               ("in2", 6, 8), ("out2", 4, 8), ("up2", 22, 8), ("down2", 4, 22)]
FIRST, GROUPS, CHUNKS = {}, {}, {}
_n = 0
for _name, _g, _c in PROJECTIONS:
    FIRST[_name], GROUPS[_name], CHUNKS[_name] = _n, _g, _c
    _n += _g * _c
N_CHUNKS = _n
RING = 4

VEC = {}
_n = 0
for _name, _w in [("g_pre_mix", KT), ("g_post_mix", KT), ("g_pre_ffn", KT), ("g_post_ffn", KT),
                  ("norm0", KT), ("norm1", KT), ("norm2", KT), ("norm3", KT), ("mu", 28), ("w0", RT),
                  ("a0", RT), ("k_k", RT), ("k_a", RT), ("r_k", RT), ("ln_w", RT), ("ln_b", RT),
                  ("conv_w", 3 * RT), ("conv_ffn", 3 * FT), ("conv_ffn2", 6 * FT)]:
    VEC[_name] = _n
    _n += _w
N_VEC = _n

C = 64
CHUNK_LENGTHS = [64, 64, 64, 64, 16]
LEVELS = [6, 6, 6, 6, 4]


class Count:

    def __init__(self):
        self.n = 0

    def add(self):
        self.n = self.n + 1
        return self.n

    def enter(self, i, first, per_turn):
        self.start, self.per_turn = self.n, per_turn
        self.n = i * per_turn + (self.n - first * per_turn)

    def leave(self, turns):
        self.n = self.start + turns * self.per_turn


def program(nc, d):
    with ExitStack() as ctx:
        def sem(name):
            return ctx.enter_context(nc.semaphore(name))

        base = [0]

        def at(name, shape, dt, offset):
            with ExitStack() as s:
                if offset:
                    s.enter_context(nc.sbuf_tensor(name + "_below", [P, offset // 4], F32))
                return s.enter_context(nc.sbuf_tensor(name, shape, dt))

        def persistent(name, shape, dt=F32):
            t = at(name, shape, dt, base[0])
            size = 4 * int(np.prod(shape[1:]))
            base[0] += -(-size // 32) * 32
            return t

        raw = persistent("raw", [P, RING, 2, 512])
        wh = persistent("wh", [P, RING, 2, 512], F32R)
        wl = persistent("wl", [P, RING, 2, 512], F32R)
        vec = persistent("vec", [P, N_VEC])
        ident = persistent("ident", [P, P])
        ones = persistent("ones", [P, P])
        bones = persistent("bones", [P, P])
        rstd = persistent("rstd", [P, L])
        rstd_post = persistent("rstd_post", [P, L])
        LENT = base[0] - 4 * L
        sq = persistent("sq", [P, 2, L])
        sq_sum = persistent("sq_sum", [P, L])
        sq_last = persistent("sq_last", [P, 4, L])
        root = at("root", [P, L], F32, base[0] - 4 * L)
        eps = persistent("eps", [P, 1])
        gn_eps = persistent("gn_eps", [P, 1])
        R = base[0]

        def region(name, shape, offset, dt=F32):
            return at(name, shape, dt, R + offset)

        h = region("h", [P, KT, L], 0)
        xh = region("xh", [P, KT, L], 17408, F32R)
        xl = region("xl", [P, KT, L], 34816, F32R)
        z = region("z", [P, 28, L + 1], 52224)
        ych = region("ych", [P, RT, LG], 82816, F32R)
        ycl = region("ycl", [P, RT, LG], 91072, F32R)
        cg = region("cg", [P, 4, LG + 2], 99328)
        hg = region("hg", [P, 4, LG + 2], 103488)
        cc = region("cc", [P, 4, LG], 107648)
        bg = region("bg", [P, 4, LG], 111776)
        zd = region("zd", [P, 4, L], 115904)
        wdu = region("wdu", [LORA, RW], 154496)
        aup = region("aup", [LORA, RW], 124416)
        gup = region("gup", [P, 2, RW], 128512)
        rkr = region("rkr", [P, RT, L], 136704)
        tw = region("tw", [P, L], 145408)
        sgd = region("sgd", [P, 2, L], 146496)
        reset = region("reset", [P, L], 148672)
        table = region("table", [32, N_HEADS], 149760)
        onehot = region("onehot", [32, 384], 149888)
        maskrow = region("maskrow", [32, 384], 151424)
        erow = region("erow", [32, 384], 152960)
        lmask = region("lmask", [P, 6, P], 160768)
        gmask = region("gmask", [P, 2, C], 163840)
        b_ = region("b", [P, RT, L], 0)
        kn = region("kn", [P, RT, L], 8704)
        cum = region("cum", [P, RT, L], 17408)
        bonus = region("bonus", [P, RT, L], 26112)
        gate = region("gate", [P, RT, L], 34816)
        pe1 = region("pe1", [P, RT, C + 1], 43520)
        pinv = region("pinv", [P, RT, C], 45600)
        sw = region("sw", [P, RT, L], 119296)
        _o = [99328]

        def chunk_buffer(name, width=P):
            t = region(name, [P, RT, width], _o[0])
            _o[0] += 4 * RT * width
            return t

        HALF_TILES = RT // 2
        ar = [chunk_buffer("ar0", 2 * P), chunk_buffer("ar1", 2 * P)]
        bkf, bkt = chunk_buffer("bkf"), chunk_buffer("bkt")
        xuv = [chunk_buffer("xuv0"), chunk_buffer("xuv1")]
        ga = chunk_buffer("ga")
        gr = [chunk_buffer("gr0"), chunk_buffer("gr1")]
        tt = chunk_buffer("tt")
        am = [chunk_buffer("am0"), chunk_buffer("am1")]
        st = chunk_buffer("st")
        tn = at("tn", [P, RT, P], F32, LENT)
        qb = at("qb", [P, RT, P], F32, LENT + 4 * RT * P)
        vd = region("vd", [P, RT, P], 47648)
        zb = region("zb", [P, RT, P], 52224)
        pend = region("pend", [P, len(CHUNK_LENGTHS), RT], 164352)
        yrh = region("yrh", [P, RT, LG], 99328, F32R)
        yrl = region("yrl", [P, RT, LG], 107584, F32R)
        yc = region("yc", [P, RT, LG], 17408)
        yc2 = region("yc2", [P, RT, LG], 0)
        mix = region("mix", [P, KT, LG], 116000)
        gt = region("gt", [P, 4, LG], 52224)
        cv = region("cv", [P, 4, SEQ], 56352)
        sg = region("sg", [P, 4, SEQ], 60448)
        ut = region("ut", [P, 4, SEQ], 64544)
        av = region("av", [P, 4, SEQ], 68640)
        acth = region("acth", [P, FT, SEQ], 73216, F32R)
        actl = region("actl", [P, FT, SEQ], 118272, F32R)
        mixf = region("mixf", [P, KT, SEQ], 52224)
        qf = region("qf", [P, KT, SEQ], 52224)
        kf = region("kf", [P, 4, SEQ], 68608)
        vf = region("vf", [P, 4, SEQ], 72704)
        vt = region("vt", [P, 2, 512], 76800)
        bias = region("bias", [P, N_HEADS, SEQ], 80896)
        y2h = region("y2h", [P, KT, SEQ], 113664, F32R)
        y2l = region("y2l", [P, KT, SEQ], 130048, F32R)
        SLOTS = 4
        sc = region("sc", [P, SLOTS, 384], 146432)
        pr = region("pr", [P, SLOTS, 384], 152576)
        pt = region("pt", [P, 2, 3, 4, QB], 17408)
        _o = [R + 164864]
        stats = []
        for name in ("rowmax", "negmax", "rowsum", "esink", "denom", "rdenom"):
            stats.append(at(name, [P, SLOTS, 2], F32, _o[0]))
            _o[0] += 32
        rowmax, negmax, rowsum, esink, denom, rdenom = stats
        sinks = region("sinks", [P, N_HEADS], 158720)
        mix2 = region("mix2", [P, KT, SEQ], 52224)

        ps = ctx.enter_context(nc.psum_tensor("ps", [P, 8, 512], F32))

        landed = [sem(f"landed{i}") for i in range(RING)]
        high_ready, low_ready, chunk_used = sem("high_ready"), sem("low_ready"), sem("chunk_used")
        vec_landed, consts, h_again, lora_landed = sem("vec_landed"), sem("consts"), sem("h_again"), sem("lora_landed")
        h_landed = [sem(f"h_landed{i}") for i in range(4)]
        bias_stored, bias_landed, erow_ready, sinks_landed = (sem("bias_stored"), sem("bias_landed"),
                                                              sem("erow_ready"), sem("sinks_landed"))
        bias_mm = sem("bias_mm")
        x_high, x_low, h_ready = sem("x_high"), sem("x_low"), sem("h_ready")
        sq_ready, sq_added = sem("sq_ready"), sem("sq_added")
        last_sq, scaled_ready, eps_ready = sem("last_sq"), sem("scaled_ready"), sem("eps_ready")
        ss_done, root_ready, rstd_ready = sem("ss_done"), sem("root_ready"), sem("rstd_ready")
        group_read = sem("group_read")
        cv_ready, sg_ready, av_ready, act_high, act_low = (sem("cv_ready"), sem("sg_ready"), sem("av_ready"),
                                                           sem("act_high"), sem("act_low"))
        dve_step, z_edge_zero = sem("dve_step"), sem("z_edge_zero")
        yv_ready, y_high, y_low = sem("yv_ready"), sem("y_high"), sem("y_low")
        z_ready = sem("z_ready")
        stored = sem("stored")
        pre_act, pre_dve, pre_pe = sem("pre_act"), sem("pre_dve"), sem("pre_pe")
        exp_ready, fac_ready, bk_ready, vd_ready, zeroed = (sem("exp_ready"), sem("fac_ready"), sem("bk_ready"),
                                                            sem("vd_ready"), sem("zeroed"))
        gram_done, bk_turned, bkt_ready, v_done, v_ready = (sem("gram_done"), sem("bk_turned"), sem("bkt_ready"),
                                                            sem("v_done"), sem("v_ready"))
        am_ready, am_turned, q_done, q_ready, d_done, tt_ready = (sem("am_ready"), sem("am_turned"), sem("q_done"),
                                                                  sem("q_ready"), sem("d_done"), sem("tt_ready"))
        z_done, zb_ready, u_done, x_ready, s_done, st_ready, y_done, y_ready = (
            sem("z_done"), sem("zb_ready"), sem("u_done"), sem("x_ready"), sem("s_done"), sem("st_ready"),
            sem("y_done"), sem("y_ready"))
        end_factors = sem("end_factors")
        v_turned, vt_ready = sem("v_turned"), sem("vt_ready")
        s_ready, sc_ready, max_ready, p_ready, pn_ready = (sem("s_ready"), sem("sc_ready"), sem("max_ready"),
                                                           sem("p_ready"), sem("pn_ready"))
        p_turned, pt_ready, o_done, o_high, o_low = (sem("p_turned"), sem("pt_ready"), sem("o_done"),
                                                     sem("o_high"), sem("o_low"))

        G0, n = {}, 0
        for name, groups, _ in PROJECTIONS:
            G0[name] = n
            n += groups

        scratch = nc.dram_tensor("bias_rows", [N_HEADS, 384], F32, kind="Internal").ap()

        def vcol(name, i):
            return vec[:, bass.ds(VEC[name] + i, 1)]

        def over(ap, tiles):
            return ap.unsqueeze(1).broadcast_to([ap.shape[0], tiles, ap.shape[1]])

        SUMS = [("w_in", L), ("w_out", LG), ("gate_up", LG), ("down", SEQ),
                ("in2", SEQ), ("out2", SEQ), ("up2", SEQ), ("down2", SEQ)]
        SUM = {name: s for s, (name, _) in enumerate(SUMS)}
        TOKENS = dict(SUMS)
        OUTPUTS = ("w_out", "down", "out2", "down2")
        SQUARES = {name: KT - 4 if name in OUTPUTS else KT for name in SUM}
        SQ0 = {name: sum(SQUARES[x] for x, _ in SUMS[:s]) for name, s in SUM.items()}

        def sum_parts(name):
            n = TOKENS[name]
            if name in OUTPUTS:
                return [(0, 0, 0, n)]
            first = min(n, 512 - n)
            return [(0, n, 0, first)] + ([(1, n, first, n - first)] if first < n else [])
        XSPLIT = {"w_in": 0, "gate_up": 1, "in2": 2, "up2": 3}
        PAIRS = D_FF // 512

        N_RC = len(CHUNK_LENGTHS)
        T0 = [sum(CHUNK_LENGTHS[:c]) for c in range(N_RC)]

        def nth(c, half=1):
            return 2 * c + half + 1

        def level(c, l, half=1):
            return 2 * (sum(LEVELS[:c]) + l) + half + 1

        def inner(c, l, half=1):
            return 2 * (sum(LEVELS[:c]) - c + l - 1) + half + 1

        def u_zero(c):
            return 4 * min(c + 1, 2) + 2 * max(c - 1, 0)

        def tiles(t, half):
            return t[:, HALF_TILES * half:HALF_TILES * (half + 1)]

        def bank(b):
            return ps[:, b, :].rearrange("p (f t) -> p f t", f=HALF_TILES)

        HEAD_ROWS = [slice(0, HEAD), slice(HEAD, P)]

        block = ctx.enter_context(nc.Block())

        @block.sync
        def _(sp):
            for name, groups, chunks in PROJECTIONS:
                weights = d[name]
                first = FIRST[name]
                if first == 0:
                    for j in range(RING):
                        if j == 1:
                            sp.wait_ge(h_landed[0], 16)
                        sp.dma_start(raw[:, j], weights[j]).then_inc(landed[j], 16)
                start = 1 if first == 0 else 0
                with sp.Fori(start, groups * chunks // RING) as i:
                    for j in range(RING):
                        sp.wait_ge(low_ready, i * RING + (first + j - RING + 1))
                        sp.dma_start(raw[:, j], weights[i * RING + j]).then_inc(landed[j], 16)
            for k in range(0, KT, 4):
                sp.wait_ge(h_ready, 16 * 3 + k + 4)
                sp.dma_start(d["out"][:, k:k + 4, :], h[:, k:k + 4, TU:L]).then_inc(stored, 16)
            sp.wait_ge(stored, 16 * 4)

        @block.gpsimd
        def _(pool):
            pool.memset(z[:, :, 0:1], 0.0).then_inc(z_edge_zero, 1)

            pool.wait_ge(z_edge_zero, 1)
            pool.memset(gn_eps[:], GN_EPS).then_inc(eps_ready, 1)
            pool.wait_ge(eps_ready, 1)
            pool.memset(eps[:], RMS_EPS).then_inc(eps_ready, 1)
            pool.wait_ge(eps_ready, 2)

            for s, (name, n) in enumerate(SUMS):
                q0 = SQ0[name]

                def add(k, slot):
                    pool.wait_ge(sq_ready, q0 + k + 1)
                    pool.wait_ge(sq_added, q0 + k)
                    pool.tensor_tensor(sq_sum[:, 0:n], sq_sum[:, 0:n], sq[:, slot, 0:n], ALU.add).then_inc(sq_added, 1)

                source = {"gate_up": mix, "in2": mixf, "up2": mix2}.get(name)

                def scale(k):
                    tile = source[:, bass.ds(k, 1), 0:n].rearrange("p k n -> p (k n)")
                    pool.tensor_tensor(tile, tile, rstd_post[:, 0:n], ALU.mult).then_inc(scaled_ready, 1)

                if source is not None:
                    pool.wait_ge(rstd_ready, s)
                    scale(1)
                    scale(3)
                pool.wait_ge(sq_ready, q0 + 1)
                if s:
                    pool.wait_ge(ss_done, s)
                pool.tensor_copy(sq_sum[:, 0:n], sq[:, 0, 0:n]).then_inc(sq_added, 1)
                add(1, 1)
                if source is None:
                    with pool.Fori(1, SQUARES[name] // 2) as i:
                        add(2 * i, 0)
                        add(2 * i + 1, 1)
                else:
                    with pool.Fori(1, KT // 2 - 1) as i:
                        scale(2 * i + 3)
                        add(2 * i, 0)
                        add(2 * i + 1, 1)
                    add(KT - 2, 0)
                    add(KT - 1, 1)
                if s:
                    continue
                pool.wait_ge(pre_dve, 7)
                n_zeroed = 0
                for c, n in enumerate(CHUNK_LENGTHS):
                    t0, short = T0[c], n < C
                    if c >= 2:
                        pool.wait_ge(y_done, nth(c - 2))
                        pool.wait_ge(s_done, nth(c - 2))
                    for own in (True, False) if c < 2 else (True,):
                        for e in range(2):
                            if n_zeroed:
                                pool.wait_ge(zeroed, n_zeroed)
                            cols = slice(64 * e, 64 * e + 64) if own else slice(64 - 64 * e, 128 - 64 * e)
                            pool.memset(xuv[c % 2][HEAD_ROWS[e], :, cols], 0.0).then_inc(zeroed, 1)
                            n_zeroed += 1
                    if short:
                        pool.wait_ge(zeroed, u_zero(c))
                        pool.memset(ar[c % 2][:], 0.0).then_inc(zeroed, 1)
                        pool.wait_ge(zeroed, u_zero(c) + 1)
                    pool.wait_ge(exp_ready, 2 * c + 2)
                    if c:
                        pool.wait_ge(bk_turned, nth(c - 1))
                    if short:
                        pool.memset(bkf[:], 0.0).then_inc(zeroed, 1)
                    pool.wait_ge(zeroed, u_zero(c) + 2 * short)
                    for e in range(2):
                        rows = HEAD_ROWS[e]
                        pool.tensor_tensor(bkf[rows, :, 64 * e:64 * e + n], b_[rows, :, t0:t0 + n], pinv[rows, :, 0:n],
                                           ALU.mult).then_inc(bk_ready, 1)
                        pool.wait_ge(bk_ready, 4 * c + 2 * e + 1)
                        pool.tensor_tensor(bkf[rows, :, 64 - 64 * e:64 - 64 * e + n], z[rows, 12:20, 1 + t0:1 + t0 + n],
                                           pinv[rows, :, 0:n], ALU.mult).then_inc(bk_ready, 1)
                        pool.wait_ge(bk_ready, 4 * c + 2 * e + 2)
                    if short:
                        pool.wait_ge(v_done, nth(c - 1))
                        pool.memset(vd[:], 0.0).then_inc(zeroed, 1)
                    if c == 1:
                        pool.wait_ge(pre_act, 23)
                        for f in range(RT):
                            pool.tensor_scalar(bonus[:, f], bonus[:, f], vcol("ln_b", f), None, ALU.add).then_inc(end_factors, 1)
                            pool.wait_ge(end_factors, f + 1)
                        pool.tensor_tensor(bonus[:], bonus[:], gate[:], ALU.mult).then_inc(end_factors, 1)
                        pool.wait_ge(end_factors, RT + 1)
                        for f in range(RT):
                            pool.tensor_scalar(gate[:, f], gate[:, f], vcol("ln_w", f), None, ALU.mult).then_inc(end_factors, 1)
                            pool.wait_ge(end_factors, RT + f + 2)
            pool.wait_ge(rstd_ready, len(SUMS))
            for k in range(1, KT, 2):
                pool.tensor_tensor(mixf[:, k], mixf[:, k], rstd_post[:, 0:SEQ], ALU.mult).then_inc(scaled_ready, 1)

        @block.scalar
        def _(act):

            def high(n, slot):
                if not isinstance(n, int):
                    act.wait_ge(landed[slot], (n - slot) * (16 // RING) + 16)
                    act.wait_ge(chunk_used, n - (RING - 1))
                else:
                    act.wait_ge(landed[slot], 16 * (n // RING + 1))
                    if n >= RING:
                        act.wait_ge(chunk_used, n - RING + 1)
                act.activation(wh[:, slot], raw[:, slot], ACT.Copy).then_inc(high_ready, 1)

            def highs(first, count, slot=0):
                for c in range(count):
                    high(first + c, (slot + c) % RING)

            def clamp(first, count):
                return max(0, min(count, N_CHUNKS - first))

            def square(src, index, n):
                if index >= 2:
                    act.wait_ge(sq_added, index - 1)
                act.activation(sq[:, index % 2, 0:n], src, ACT.Square).then_inc(sq_ready, 1)

            def take_root(name):
                act.wait_ge(ss_done, SUM[name] + 1)
                for b, col, t, n in sum_parts(name):
                    last = act.activation(root[:, t:t + n], ps[:, b, col:col + n], ACT.Sqrt, scale=1.0 / D, bias=eps[:, 0:1])
                last.then_inc(root_ready, 1)

            def x_tile(name, k, t0, gain):
                n = TOKENS[name]
                act.activation(xh[:, k, 0:n], h[:, k, t0:t0 + n], ACT.Copy, scale=vcol(gain, k)).then_inc(x_high, 1)
                square(h[:, k, t0:t0 + n], SQ0[name] + k, n)

            def opening(name, tile):
                first = FIRST[name]
                for c in range(8):
                    tile(2 * c)
                    tile(2 * c + 1)
                    if c < 3 and first == 0:
                        highs(1 + c, 1, 1 + c)
                    if c >= 3:
                        highs(first + 4 + c - 3, 1, (c - 3) % RING)
                highs(first + 9, 3, 1)
                take_root(name)

            def mix_group(name, g, src, n):
                if g == 3:
                    act.wait_ge(chunk_used, FIRST[name] + 4 * CHUNKS[name])
                    for k in range(4):
                        act.activation(sq_last[:, k, 0:n], ps[:, 4 + k, 0:n], ACT.Square).then_inc(last_sq, 1)
                    return
                act.wait_ge(group_read, G0[name] + g + 1)
                for k in range(4 * g, 4 * g + 4):
                    square(src[:, k, :], SQ0[name] + k, n)

            def plain(name, evacuate, skip_first=False, stops={}, ahead=0):
                first, per = FIRST[name], CHUNKS[name]
                for g in range(1 if skip_first else 0, GROUPS[name]):
                    start = first + g * per + RING
                    count = clamp(start, per)
                    if g == 0:
                        start, count = start + ahead, count - ahead
                    head = min(count, 1)
                    highs(start, head, start % RING)
                    if g and g - 1 not in stops:
                        evacuate(g - 1)
                    if count - head > 8:
                        more(start + head, count - head)
                    else:
                        highs(start + head, count - head, (start + head) % RING)
                    if g in stops:
                        evacuate(g)
                        stops[g]()
                evacuate(GROUPS[name] - 1)

            def more(first, count):
                slot = first % RING
                with act.Fori(0, count // RING) as i:
                    highs(i * RING + first, RING, slot)
                highs(first + count // RING * RING, count % RING, slot)

            act.dma_start(vec[:], d["vec"]).then_inc(vec_landed, 16)
            for k in range(0, KT, 4):
                act.dma_start(h[:, k:k + 4, :], d["ht"][:, k:k + 4, :]).then_inc(h_landed[k // 4], 16)
            for dst, src in ((ident, "ident"), (ones, "ones"), (bones, "bones"), (table, "table"), (onehot, "onehot"),
                             (maskrow, "maskrow")):
                act.dma_start(dst[:], d[src]).then_inc(consts, 16)
            for dst, src in ((wdu, "wdu"), (aup, "aup"), (gup, "gup"), (reset, "reset"), (lmask, "lmask"),
                             (gmask, "gmask")):
                act.dma_start(dst[:], d[src]).then_inc(lora_landed, 16)
            act.wait_ge(vec_landed, 16)
            highs(0, 1)
            act.wait_ge(eps_ready, 2)

            def first_tile(k):
                act.wait_ge(h_landed[k // 4], 16)
                x_tile("w_in", k, 0, "g_pre_mix")

            opening("w_in", first_tile)
            act.wait_ge(erow_ready, 1)
            act.dma_start(scratch, erow[:]).then_inc(bias_stored, 16)

            def evacuate_in(g):
                if g in (9, 12):
                    half = (g - 9) // 3
                    act.wait_ge(yv_ready, half + 1)
                    act.activation(ych[:, 4 * half:4 * half + 4], bg[:], ACT.Copy).then_inc(y_high, 1)

            def rates():
                act.wait_ge(z_ready, 1)
                act.activation(tw[:], z[:, 0, 1:L + 1], ACT.Tanh).then_inc(pre_act, 1)
                act.activation(sgd[:], z[:, 2:4, 1:L + 1], ACT.Sigmoid).then_inc(pre_act, 1)
                for f in range(RT):
                    act.wait_ge(pre_pe, 1 + f // 4)
                    act.activation(b_[:, f], ps[:, (4 + f) % 8, 0:L], ACT.Sigmoid, bias=vcol("a0", f)).then_inc(pre_act, 1)
                act.wait_ge(z_ready, 7)
                for f in range(RT):
                    act.wait_ge(pre_pe, 3 + f // 4)
                    act.activation(sw[:, f], ps[:, (4 + f) % 8, 0:L], ACT.Sigmoid, bias=vcol("w0", f)).then_inc(pre_act, 1)

            def lengths():
                act.wait_ge(pre_dve, 1)
                act.activation(rkr[:], kn[:], ACT.Square).then_inc(pre_act, 1)
                for half in range(2):
                    act.wait_ge(pre_pe, 5 + half)
                    act.activation(tiles(rkr, half), ps[:, 4 - 4 * half:8 - 4 * half, 0:L], ACT.Sqrt).then_inc(pre_act, 1)

            plain("w_in", evacuate_in, skip_first=True, stops={6: rates, 8: lengths})
            for half in range(2):
                act.wait_ge(pre_pe, 7 + half)
                act.activation(tiles(gate, half), ps[:, 4 - 4 * half:8 - 4 * half, 0:L], ACT.Copy).then_inc(pre_act, 1)

            def decays(c):
                n, t0 = CHUNK_LENGTHS[c], T0[c]
                if c:
                    act.wait_ge(fac_ready, c)
                    act.wait_ge(bk_ready, 4 * c)
                act.activation(pe1[:, :, 1:n + 1], cum[:, :, t0:t0 + n], ACT.Exp, scale=-DECAY_SCALE).then_inc(exp_ready, 1)
                act.activation(pinv[:, :, 0:n], cum[:, :, t0:t0 + n], ACT.Exp, scale=DECAY_SCALE).then_inc(exp_ready, 1)
                if c:
                    act.wait_ge(v_done, nth(c - 1))
                if n < C:
                    act.wait_ge(zeroed, u_zero(c) + 3)
                act.activation(vd[:, :, :].rearrange("p f (e t) -> p f e t", e=2)[:, :, :, 0:n],
                               z[:, 20:28, 1 + t0:1 + t0 + n].unsqueeze(2).broadcast_to([P, RT, 2, n]),
                               ACT.Copy).then_inc(vd_ready, 1)

            act.wait_ge(pre_dve, 4)
            decays(0)
            for c in range(N_RC + 1):
                if c:
                    for half in range(2):
                        act.wait_ge(z_done, nth(c - 1, half))
                        act.activation(tiles(zb, half), bank(6 + half), ACT.Copy).then_inc(zb_ready, 1)
                    for half in range(2):
                        act.wait_ge(u_done, nth(c - 1, half))
                        for e in range(2):
                            act.activation(tiles(xuv[(c - 1) % 2], half)[HEAD_ROWS[e], :, 64 * e:64 * e + 64],
                                           bank(6 + half)[HEAD_ROWS[e], :, 64 * e:64 * e + 64],
                                           ACT.Copy).then_inc(x_ready, 1)
                if c < N_RC:
                    for half in range(2):
                        act.wait_ge(bk_turned, nth(c, half))
                        if c:
                            act.wait_ge(s_done, nth(c - 1))
                        act.activation(tiles(bkt, half), bank(4 + half), ACT.Copy).then_inc(bkt_ready, 1)
                if c:
                    n, t0 = CHUNK_LENGTHS[c - 1], T0[c - 1]
                    for half in range(2):
                        act.wait_ge(y_done, nth(c - 1, half))
                        for e in range(2):
                            act.activation(z[HEAD_ROWS[e], 4 + 4 * half:8 + 4 * half, 1 + t0:1 + t0 + n],
                                           bank(half)[HEAD_ROWS[e], :, 64 * e:64 * e + n], ACT.Copy).then_inc(y_ready, 1)
                if c == N_RC:
                    continue
                for half in range(2):
                    act.wait_ge(v_done, nth(c, half))
                    act.wait_ge(zeroed, u_zero(c))
                    for e in range(2):
                        rows = HEAD_ROWS[1 - e]
                        act.activation(tiles(xuv[c % 2], half)[rows, :, 64 * e:64 * e + 64],
                                       bank(4 + half)[rows, :, 64 * e:64 * e + 64], ACT.Copy).then_inc(v_ready, 1)
                for l in range(1, LEVELS[c]):
                    for half in range(2):
                        act.wait_ge(q_done, inner(c, l, half))
                        act.activation(tiles(qb, half), bank(half), ACT.Copy).then_inc(q_ready, 1)
                    if l == 1 and c + 1 < N_RC:
                        decays(c + 1)
            act.wait_ge(pre_dve, 8)
            act.activation(yc2[:], yc[:], ACT.Square).then_inc(pre_act, 1)
            for half in range(2):
                act.wait_ge(pre_pe, 12 + half)
                act.activation(tiles(yc2, half), ps[:, 4 * half:4 * half + 4, 0:LG], ACT.Sqrt, scale=1.0 / HEAD,
                               bias=gn_eps[:, 0:1]).then_inc(pre_act, 1)
            highs(FIRST["w_out"] + 4, 1)
            for half in range(2):
                act.wait_ge(pre_dve, 9 + half)
                act.activation(tiles(yrh, half), tiles(yc, half), ACT.Copy).then_inc(y_high, 1)
                highs(FIRST["w_out"] + 5 + half, 1, 1 + half)
            highs(FIRST["w_out"] + 7, 1, 3)
            act.dma_start(h[:], d["ht"]).then_inc(h_again, 16)

            plain("w_out", lambda g: mix_group("w_out", g, mix, LG), ahead=4)
            take_root("w_out")

            def residual_tile(name, k, t0, gain, base):
                act.wait_ge(h_ready, base + k + 1)
                x_tile(name, k, t0, gain)

            def feed_forward(name, block2):
                first = FIRST[name]
                P0 = PAIRS if block2 else 0

                def gated(p):
                    if not (isinstance(p, int) and p + P0 == 0):
                        act.wait_ge(av_ready, p + P0)
                    act.wait_ge(cv_ready, p + P0 + 1)
                    act.activation(sg[:], cv[:], ACT.Silu).then_inc(sg_ready, 1)

                def activated(p):
                    act.wait_ge(av_ready, p + P0 + 1)
                    act.activation(acth[:, bass.ds(p * 4, 4), :], av[:], ACT.Copy).then_inc(act_high, 1)

                def pair(p):
                    highs(p * 16 + (first + 12), 3)
                    gated(p)
                    highs(p * 16 + (first + 15), 9, 3)
                    activated(p)
                    highs(p * 16 + (first + 24), 4)

                pair(0)
                with act.Fori(1, PAIRS - 1) as p:
                    pair(p)
                last = first + 16 * PAIRS - 4
                highs(last, 3)
                gated(PAIRS - 1)
                highs(last + 3, 5, 3)
                activated(PAIRS - 1)

            opening("gate_up", lambda k: residual_tile("gate_up", k, TG, "g_pre_ffn", 0))
            feed_forward("gate_up", False)
            plain("down", lambda g: mix_group("down", g, mixf, SEQ))
            take_root("down")

            opening("in2", lambda k: residual_tile("in2", k, TU, "norm0", 16))
            act.dma_start(sinks[:], d["sinks"]).then_inc(sinks_landed, 16)
            act.wait_ge(bias_stored, 16)
            act.wait_ge(x_high, 48)
            bias_src = bass.AP(scratch.tensor, 0, [[1, P], [384, N_HEADS], [1, SEQ]])
            act.dma_start(bias[:], bias_src).then_inc(bias_landed, 16)
            plain("in2", lambda g: None, skip_first=True)

            def softmax_head(i):
                s = i % SLOTS
                act.wait_ge(max_ready, i + 1)
                if i >= SLOTS:
                    act.wait_ge(p_turned, i - SLOTS + 1)
                act.activation(pr[:, s, 0:QB], sc[:, s, 0:QB], ACT.Exp, bias=negmax[:, s, 0:1],
                               accum_out=rowsum[:, s, 0:1])
                act.activation(pr[:, s, QB:384], sc[:, s, QB:384], ACT.Exp, bias=negmax[:, s, 1:2],
                               accum_out=rowsum[:, s, 1:2])
                act.activation(esink[:, s, :], negmax[:, s, :], ACT.Exp, bias=sinks[:, head(i):head(i) + 1]).then_inc(p_ready, 1)

            def turn_out(i):
                grp, j = divmod(i, 4)
                act.wait_ge(p_turned, i + 1)
                if grp >= 2:
                    act.wait_ge(o_done, grp - 1)
                act.activation(pt[:, grp % 2, :, j, :], ps[:, 2 + i % 2, 0:384].rearrange("p (c q) -> p c q", c=3),
                               ACT.Copy).then_inc(pt_ready, 1)

            def out_high(grp):
                g2, e = divmod(grp, 2)
                act.wait_ge(o_done, grp + 1)
                rows = slice(64 * e, 64 * e + 64)
                for b in range(2):
                    act.activation(y2h[rows, 4 * g2:4 * g2 + 4, b * QB:(b + 1) * QB],
                                   ps[rows, 4 + 2 * (grp % 2) + b, :].rearrange("p (j q) -> p j q", j=4),
                                   ACT.Copy).then_inc(o_high, 1)

            def head(i):
                g2, e, j = i // 8, i // 4 % 2, i % 4
                return 4 * (2 * g2 + e) + j

            act.wait_ge(sinks_landed, 16)
            act.wait_ge(v_turned, 1)
            act.activation(vt[:], ps[:, 0:2, :], ACT.Copy).then_inc(vt_ready, 1)
            for i in range(N_HEADS + 6):
                if i < N_HEADS:
                    softmax_head(i)
                if 4 <= i < N_HEADS + 4:
                    turn_out(i - 4)
                if i >= 9 and (i - 9) % 4 == 0:
                    out_high((i - 9) // 4)
            plain("out2", lambda g: mix_group("out2", g, mix2, SEQ))
            take_root("out2")
            opening("up2", lambda k: residual_tile("up2", k, TU, "norm2", 32))
            feed_forward("up2", True)
            plain("down2", lambda g: mix_group("down2", g, mixf, SEQ))
            take_root("down2")

        @block.vector
        def _(dve):
            steps = Count()

            def low(n, slot):
                dve.wait_ge(high_ready, n + 1)
                dve.tensor_tensor(wl[:, slot], raw[:, slot], wh[:, slot].bitcast(F32), ALU.subtract).then_inc(low_ready, 1)

            def lows(first, count, slot=0):
                for c in range(count):
                    low(first + c, (slot + c) % RING)

            def clamp(first, count):
                return max(0, min(count, N_CHUNKS - first))

            def more(first, count):
                slot = first % RING
                with dve.Fori(0, count // RING) as i:
                    lows(i * RING + first, RING, slot)
                lows(first + count // RING * RING, count % RING, slot)

            def inverse_root(name, dst):
                s, n = SUM[name], TOKENS[name]
                dve.wait_ge(root_ready, s + 1)
                dve.reciprocal(dst[:, 0:n], root[:, 0:n]).then_inc(rstd_ready, 1)
                dve.wait_ge(rstd_ready, s + 1)

            def x_low_tile(name, k, t0, gain):
                n = TOKENS[name]
                dve.wait_ge(x_high, 16 * XSPLIT[name] + k + 1)
                dve.scalar_tensor_tensor(xl[:, k, 0:n], h[:, k, t0:t0 + n], vcol(gain, k), xh[:, k, 0:n].bitcast(F32),
                                         ALU.mult, ALU.subtract).then_inc(x_low, 1)

            def opening(name, tile, finish):
                first = FIRST[name]
                for c in range(8):
                    tile(2 * c)
                    tile(2 * c + 1)
                    if c == 7:
                        finish()
                    if c < 3 and first == 0:
                        lows(1 + c, 1, 1 + c)
                    if c >= 3:
                        lows(first + 4 + c - 3, 1, (c - 3) % RING)
                lows(first + 9, 3, 1)
                inverse_root(name, rstd)

            def plain(name, evacuate, skip_first=False, stops={}, middles={}, ahead=0):
                first, per = FIRST[name], CHUNKS[name]
                for g in range(1 if skip_first else 0, GROUPS[name]):
                    start = first + g * per + RING
                    count = clamp(start, per)
                    if g == 0:
                        start, count = start + ahead, count - ahead
                    head = min(count, 1)
                    lows(start, head, start % RING)
                    if g and g - 1 not in stops:
                        evacuate(g - 1)
                    if count - head > 8:
                        more(start + head, count - head)
                    elif g in middles:
                        lows(start + head, 3, (start + head) % RING)
                        middles[g]()
                        lows(start + head + 3, count - head - 3, (start + head + 3) % RING)
                    else:
                        lows(start + head, count - head, (start + head) % RING)
                    if g in stops:
                        evacuate(g)
                        stops[g]()
                evacuate(GROUPS[name] - 1)

            def group_full(name, g):
                ahead = 4 if (name, g) == ("w_out", 0) else 0
                dve.wait_ge(chunk_used, FIRST[name] + (g + 1) * CHUNKS[name] + ahead)

            def banks(g, t, n):
                b = 4 * (g % 2)
                return ps[:, b:b + 4, t:t + n]

            dve.wait_ge(vec_landed, 16)
            lows(0, 1)

            def first_tile(k):
                dve.wait_ge(h_landed[k // 4], 16)
                x_low_tile("w_in", k, 0, "g_pre_mix")

            opening("w_in", first_tile, lambda: None)
            dve.wait_ge(consts, 16 * 6)
            dve.wait_ge(bias_mm, 1)
            for b in range(2):
                last = dve.tensor_tensor(erow[:, 192 * b:192 * (b + 1)], ps[0:32, 2 + b, L:L + 192],
                                         maskrow[:, 192 * b:192 * (b + 1)], ALU.add)
            last.then_inc(erow_ready, 1)

            def evacuate_in(g):
                group_full("w_in", g)
                b = 4 * (g % 2)
                if g < 7:
                    if g == 0:
                        dve.wait_ge(z_edge_zero, 1)
                    dve.tensor_tensor(z[:, 4 * g:4 * g + 4, 1:L + 1], ps[:, b:b + 4, 0:L], over(rstd[:, 0:L], 4),
                                      ALU.mult).then_inc(group_read, 1)
                    dve.wait_ge(group_read, g + 1)
                    dve.tensor_tensor(zd[:], z[:, 4 * g:4 * g + 4, 0:L], z[:, 4 * g:4 * g + 4, 1:L + 1],
                                      ALU.subtract).then_inc(dve_step, 1)
                    t = steps.add()
                    dve.wait_ge(dve_step, t)
                    for k in range(4 * g, 4 * g + 4):
                        last = dve.scalar_tensor_tensor(z[:, k, 1:L + 1], zd[:, k % 4], vcol("mu", k), z[:, k, 1:L + 1],
                                                        ALU.mult, ALU.add)
                    last.then_inc(z_ready, 1)
                    return
                half, part = divmod(g - 7, 3)
                if part == 0:
                    dve.tensor_tensor(cg[:], ps[:, b:b + 4, 0:LG + 2], over(rstd[:, TG - 2:L], 4),
                                      ALU.mult).then_inc(group_read, 1)
                elif part == 1:
                    dve.tensor_tensor(hg[:], ps[:, b:b + 4, 0:LG + 2], over(rstd[:, TG - 2:L], 4),
                                      ALU.mult).then_inc(group_read, 1)
                    dve.wait_ge(group_read, g + 1)
                    dve.tensor_tensor(cg[:], cg[:], hg[:], ALU.mult).then_inc(dve_step, 1)
                    t = steps.add()
                    dve.wait_ge(dve_step, t)
                    t = [0] * 4
                    for j in range(4):
                        dve.tensor_scalar(cc[:, j], cg[:, j, 0:LG], vcol("conv_w", 4 * half + j), None, ALU.mult).then_inc(dve_step, 1)
                        t[j] = steps.add()
                    for tap in (1, 2):
                        for j in range(4):
                            dve.wait_ge(dve_step, t[j])
                            dve.scalar_tensor_tensor(
                                cc[:, j], cg[:, j, tap:tap + LG], vcol("conv_w", RT * tap + 4 * half + j), cc[:, j],
                                ALU.mult, ALU.add).then_inc(dve_step, 1)
                            t[j] = steps.add()
                else:
                    dve.wait_ge(dve_step, steps.n)
                    if half:
                        dve.wait_ge(y_high, half)
                    dve.tensor_tensor(bg[:], ps[:, b:b + 4, 2:LG + 2], over(rstd[:, TG:L], 4), ALU.mult).then_inc(group_read, 1)
                    dve.wait_ge(group_read, g + 1)
                    dve.tensor_tensor(bg[:], bg[:], cc[:], ALU.mult).then_inc(yv_ready, 1)
                    dve.wait_ge(yv_ready, half + 1)
                    dve.wait_ge(y_high, half + 1)
                    dve.tensor_tensor(ycl[:, 4 * half:4 * half + 4], bg[:], ych[:, 4 * half:4 * half + 4].bitcast(F32),
                                      ALU.subtract).then_inc(y_low, 1)

            def keys():
                for f in range(RT):
                    last = dve.tensor_scalar(kn[:, f], z[:, 12 + f, 1:L + 1], vcol("k_k", f), None, ALU.mult)
                last.then_inc(pre_dve, 1)

            def inverse_lengths():
                dve.wait_ge(pre_act, 21)
                dve.tensor_scalar(rkr[:], rkr[:], 1e-12, None, ALU.max).then_inc(dve_step, 1)
                dve.wait_ge(dve_step, steps.add())
                dve.reciprocal(rkr[:], rkr[:]).then_inc(dve_step, 1)
                steps.add()

            def unit_keys():
                dve.wait_ge(dve_step, steps.n)
                dve.scalar_tensor_tensor(kn[:], kn[:], -1.0, rkr[:], ALU.mult, ALU.mult).then_inc(dve_step, 1)
                steps.add()

            def keys_by_rate():
                zk = z[:, 12:20, 1:L + 1]
                dve.wait_ge(dve_step, steps.n)
                for f in range(RT):
                    dve.tensor_scalar(rkr[:, f], b_[:, f], -1.0, vcol("k_a", f), ALU.add, ALU.mult).then_inc(dve_step, 1)
                    steps.add()
                dve.wait_ge(dve_step, steps.n)
                dve.scalar_tensor_tensor(zk, rkr[:], 1.0, zk, ALU.add, ALU.mult).then_inc(dve_step, 1)
                steps.add()

            def added_keys():
                dve.wait_ge(dve_step, steps.n)
                dve.scalar_tensor_tensor(b_[:], kn[:], -1.0, b_[:], ALU.mult, ALU.mult).then_inc(dve_step, 1)
                steps.add()

            def bonus_terms():
                dve.wait_ge(dve_step, steps.n)
                for f in range(RT):
                    last = dve.scalar_tensor_tensor(rkr[:, f], z[:, 4 + f, 1:L + 1], vcol("r_k", f), z[:, 12 + f, 1:L + 1],
                                                    ALU.mult, ALU.mult)
                last.then_inc(pre_dve, 1)

            plain("w_in", evacuate_in, skip_first=True,
                  stops={6: keys, 8: lambda: None, 9: unit_keys, 10: added_keys},
                  middles={9: inverse_lengths, 10: keys_by_rate, 11: bonus_terms})
            dve.wait_ge(dve_step, steps.n)
            dve.wait_ge(lora_landed, 16 * 6)
            dve.memset(pe1[:, :, 0:1], 1.0).then_inc(pre_dve, 1)
            for f in range(RT):
                last = dve.tensor_tensor_scan(cum[:, f], reset[:], sw[:, f], 0.0, ALU.mult, ALU.add)
            last.then_inc(pre_dve, 1)
            for half in range(2):
                dve.wait_ge(pre_pe, 9 + half)
                dve.tensor_tensor(tiles(bonus, half), ps[:, 4 - 4 * half:8 - 4 * half, 0:L],
                                  z[:, 20 + 4 * half:24 + 4 * half, 1:L + 1], ALU.mult).then_inc(pre_dve, 1)
            dve.wait_ge(bias_stored, 16)
            dve.memset(st[:], 0.0).then_inc(pre_dve, 1)
            dve.wait_ge(pre_dve, 7)

            def factors(c, part, half):
                n, t0 = CHUNK_LENGTHS[c], T0[c]
                if part == 0 and half == 0:
                    dve.wait_ge(exp_ready, 2 * c + 2)
                    if c >= 2:
                        dve.wait_ge(y_done, nth(c - 2))
                    if n < C:
                        dve.wait_ge(zeroed, u_zero(c) + 1)
                    dve.tensor_copy(pend[:, c], pe1[:, :, n])
                src = kn[:, :, t0:t0 + n] if part == 0 else z[:, 4:12, 1 + t0:1 + t0 + n]
                decay = pe1[:, :, 0:n] if part == 0 else pe1[:, :, 1:n + 1]
                last = dve.tensor_tensor(
                    tiles(ar[c % 2], half).rearrange("p f (e t) -> p f e t", e=4)[:, :, 2 * part:2 * part + 2, 0:n],
                    tiles(src, half).unsqueeze(2).broadcast_to([P, HALF_TILES, 2, n]),
                    tiles(decay, half).unsqueeze(2).broadcast_to([P, HALF_TILES, 2, n]), ALU.mult)
                if part and half:
                    last.then_inc(fac_ready, 1)

            def level_matrix(c, l, half):
                if l >= 3:
                    dve.wait_ge(q_done, inner(c, l - 2, half))
                elif l == 2:
                    dve.wait_ge(am_turned, nth(c, half))
                dve.tensor_tensor(tiles(am[l % 2], half), tiles(ga, half), over(lmask[:, l], HALF_TILES),
                                  ALU.mult).then_inc(am_ready, 1)

            for part in range(2):
                for half in range(2):
                    factors(0, part, half)
            for c in range(N_RC + 1):
                if c < N_RC:
                    if c:
                        dve.wait_ge(z_done, nth(c - 1))
                    for half in range(2):
                        dve.wait_ge(gram_done, nth(c, half))
                        for part, dst in ((0, ga), (1, gr[c % 2])):
                            for e in range(2):
                                dve.tensor_tensor(tiles(dst, half)[:, :, 64 * e:64 * e + 64],
                                                  bank(2 * e + half)[:, :, 64 * part:64 * part + 64],
                                                  over(gmask[:, part], HALF_TILES), ALU.mult).then_inc(dve_step, 1)
                                steps.add()
                        dve.wait_ge(dve_step, steps.n)
                        level_matrix(c, 0, half)
                    for half in range(2):
                        dve.wait_ge(am_ready, level(c, 0, half))
                        if c:
                            dve.wait_ge(u_done, nth(c - 1, half))
                        dve.tensor_tensor(tiles(tt, half), tiles(am[0], half), over(ident[:], HALF_TILES),
                                          ALU.add).then_inc(dve_step, 1)
                        steps.add()
                        level_matrix(c, 1, half)
                if c and c < N_RC:
                    for half in range(2):
                        dve.wait_ge(s_done, nth(c - 1, half))
                        dve.wait_ge(y_done, nth(c - 1, half))
                        if c > 1:
                            dve.wait_ge(st_ready, nth(c - 2))
                        for e in range(2):
                            rows, cols = HEAD_ROWS[e], slice(64 * e, 64 * e + 64)
                            dve.tensor_tensor(tiles(st, half)[rows, :, cols], tiles(st, half)[rows, :, cols],
                                              bank(6 + half)[rows, :, cols], ALU.add).then_inc(dve_step, 1)
                            steps.add()
                        dve.wait_ge(dve_step, steps.n)
                        dve.tensor_tensor(tiles(st, half), tiles(st, half),
                                          tiles(pend[:, c - 1], half).unsqueeze(2).broadcast_to([P, HALF_TILES, P]),
                                          ALU.mult).then_inc(st_ready, 1)
                if c == N_RC:
                    continue
                for half in range(2):
                    dve.wait_ge(am_turned, nth(c, half))
                    dve.wait_ge(dve_step, steps.n)
                    dve.tensor_tensor(tiles(tn, half), bank(2 + half), over(ident[:], HALF_TILES), ALU.add).then_inc(tt_ready, 1)
                for l in range(1, LEVELS[c]):
                    for half in range(2):
                        if l + 1 < LEVELS[c]:
                            level_matrix(c, l + 1, half)
                        dve.wait_ge(tt_ready, level(c, l - 1, half))
                        dve.wait_ge(d_done, inner(c, l, half))
                        if l < LEVELS[c] - 1:
                            dve.tensor_tensor(tiles(tn, half), tiles(tn, half), bank(2 + half), ALU.add)
                        dve.tensor_tensor(tiles(tt, half), tiles(tt, half), bank(4 + half), ALU.add).then_inc(tt_ready, 1)
                        if half == 0 and l <= 4 and c + 1 < N_RC:
                            factors(c + 1, *divmod(l - 1, 2))
            dve.wait_ge(pre_pe, 11)
            zy = z[:, 4:12, 1 + TG:1 + L]
            dve.scalar_tensor_tensor(yc[:], ps[:, :, 0:LG], -1.0 / HEAD, zy, ALU.mult, ALU.add).then_inc(pre_dve, 1)
            dve.wait_ge(pre_dve, 8)
            dve.wait_ge(end_factors, 2 * RT + 1)
            dve.wait_ge(pre_act, 24)
            dve.tensor_tensor(yc[:], yc[:], gate[:, :, TG:L], ALU.mult).then_inc(dve_step, 1)
            dve.wait_ge(dve_step, steps.add())
            for half in range(2):
                dve.wait_ge(pre_act, 25 + half)
                dve.reciprocal(tiles(yc2, half), tiles(yc2, half)).then_inc(dve_step, 1)
                dve.wait_ge(dve_step, steps.add())
                dve.tensor_tensor(tiles(yc, half), tiles(yc, half), tiles(yc2, half), ALU.mult).then_inc(dve_step, 1)
                dve.wait_ge(dve_step, steps.add())
                dve.tensor_tensor(tiles(yc, half), tiles(yc, half), tiles(bonus, half)[:, :, TG:L], ALU.add).then_inc(pre_dve, 1)
                if half == 0:
                    lows(FIRST["w_out"] + 4, 1)
            for half in range(2):
                dve.wait_ge(pre_dve, 9 + half)
                dve.wait_ge(y_high, 3 + half)
                dve.tensor_tensor(tiles(yrl, half), tiles(yc, half), tiles(yrh, half).bitcast(F32), ALU.subtract).then_inc(y_low, 1)
                lows(FIRST["w_out"] + 5 + half, 1, 1 + half)
            lows(FIRST["w_out"] + 7, 1, 3)

            def mix_out(name, dst, n):
                def evacuate(g):
                    group_full(name, g)
                    if g == 3:
                        for k in range(4):
                            dve.wait_ge(last_sq, 4 * OUTPUTS.index(name) + k + 1)
                            last = dve.tensor_copy(dst[:, 4 * g + k, :], ps[:, 4 + k, 0:n])
                        last.then_inc(group_read, 1)
                        return
                    dve.tensor_copy(dst[:, 4 * g:4 * g + 4, :], banks(g, 0, n)).then_inc(group_read, 1)
                return evacuate

            plain("w_out", mix_out("w_out", mix, LG), ahead=4)
            inverse_root("w_out", rstd_post)
            dve.wait_ge(group_read, G0["gate_up"])
            dve.wait_ge(h_again, 16)

            def residual_tile(name, src, n, t0, post_gain, base):
                def tile(k):
                    if k % 2:
                        dve.wait_ge(scaled_ready, base // 2 + k // 2 + 1)
                    else:
                        dve.tensor_tensor(src[:, k, 0:n], src[:, k, 0:n], rstd_post[:, 0:n], ALU.mult).then_inc(dve_step, 1)
                        t = steps.add()
                        dve.wait_ge(dve_step, t)
                    dve.scalar_tensor_tensor(h[:, k, t0:t0 + n], src[:, k, 0:n], vcol(post_gain, k),
                                             h[:, k, t0:t0 + n], ALU.mult, ALU.add).then_inc(h_ready, 1)
                    if name and k:
                        dve.wait_ge(h_ready, base + k)
                        x_low_tile(name, k - 1, t0, {"gate_up": "g_pre_ffn", "in2": "norm0", "up2": "norm2"}[name])
                return tile

            def last_low(name, t0, gain, base):
                def finish():
                    dve.wait_ge(h_ready, base + KT)
                    x_low_tile(name, KT - 1, t0, gain)
                return finish

            def convolve(dst, tile0, taps, stride, between, done=None):
                t = [0] * 4
                for j in range(4):
                    dve.tensor_scalar(dst[:, j], gt[:, j, 0:SEQ], vcol(taps, tile0 + j), None, ALU.mult).then_inc(dve_step, 1)
                    t[j] = steps.add()
                between(0)
                for tap in (1, 2):
                    if tap == 2:
                        between(1)
                    for j in range(4):
                        dve.wait_ge(dve_step, t[j])
                        ins = dve.scalar_tensor_tensor(dst[:, j], gt[:, j, tap:tap + SEQ],
                                                       vcol(taps, tile0 + (stride * tap + j)), dst[:, j],
                                                       ALU.mult, ALU.add)
                        if done is not None and tap == 2 and j == 3:
                            ins.then_inc(done, 1)
                        else:
                            ins.then_inc(dve_step, 1)
                            t[j] = steps.add()

            def feed_forward(name, block2):
                first = FIRST[name]
                P0 = PAIRS if block2 else 0
                n = TOKENS[name]

                def gated(p):
                    def between(x):
                        lows(p * 16 + (first + 13 + x), 1, 1 + x)

                    dve.wait_ge(chunk_used, p * 16 + (first + 8))
                    if not (isinstance(p, int) and p + P0 == 0):
                        dve.wait_ge(sg_ready, p + P0)
                    off = 2 if block2 else 0
                    dve.tensor_tensor(gt[:, :, off:off + n], ps[:, 0:4, 0:n], over(rstd[:, 0:n], 4), ALU.mult).then_inc(group_read, 1)
                    dve.wait_ge(group_read, p * 2 + (G0[name] + 1))
                    convolve(cv, p * 4, "conv_ffn2" if block2 else "conv_ffn", 2 * FT if block2 else FT, between,
                             cv_ready)

                def upped(p):
                    def between(x):
                        if not isinstance(p, int) or p < PAIRS - 1:
                            lows(p * 16 + (first + 21 + x), 1, 1 + x)

                    dve.wait_ge(chunk_used, p * 16 + (first + 16))
                    if block2:
                        dve.tensor_tensor(gt[:, :, 2:2 + SEQ], ps[:, 4:8, 0:SEQ], over(rstd[:, 0:SEQ], 4),
                                          ALU.mult).then_inc(group_read, 1)
                        dve.wait_ge(group_read, p * 2 + (G0[name] + 2))
                        convolve(ut, p * 4 + FT, "conv_ffn2", 2 * FT, between)
                        dve.wait_ge(dve_step, steps.n)
                    else:
                        dve.tensor_tensor(ut[:], ps[:, 4:8, 0:SEQ], over(rstd[:, 2:2 + SEQ], 4), ALU.mult).then_inc(group_read, 1)
                        dve.wait_ge(group_read, p * 2 + (G0[name] + 2))
                        between(0)
                        between(1)
                    dve.wait_ge(sg_ready, p + P0 + 1)
                    dve.tensor_tensor(av[:], sg[:], ut[:], ALU.mult).then_inc(av_ready, 1)

                def split(p):
                    dve.wait_ge(av_ready, p + P0 + 1)
                    dve.wait_ge(act_high, p + P0 + 1)
                    dve.tensor_tensor(actl[:, bass.ds(p * 4, 4), :], av[:], acth[:, bass.ds(p * 4, 4), :].bitcast(F32),
                                      ALU.subtract).then_inc(act_low, 1)

                per_turn = 11 + (12 if block2 else 0)
                def pair(p):
                    lows(p * 16 + (first + 12), 1)
                    gated(p)
                    lows(p * 16 + (first + 15), 6, 3)
                    upped(p)
                    lows(p * 16 + (first + 23), 1, 3)
                    split(p)
                    lows(p * 16 + (first + 24), 4)

                pair(0)
                with dve.Fori(1, PAIRS - 1) as p:
                    steps.enter(p, 1, per_turn)
                    pair(p)
                    steps.leave(PAIRS - 2)
                last = first + 16 * PAIRS - 4
                lows(last, 1)
                gated(PAIRS - 1)
                lows(last + 3, 5, 3)
                upped(PAIRS - 1)
                split(PAIRS - 1)

            opening("gate_up", residual_tile("gate_up", mix, LG, TG, "g_post_mix", 0),
                    last_low("gate_up", TG, "g_pre_ffn", 0))
            feed_forward("gate_up", False)
            plain("down", mix_out("down", mixf, SEQ))
            inverse_root("down", rstd_post)
            dve.wait_ge(group_read, G0["in2"])

            opening("in2", residual_tile("in2", mixf, SEQ, TU, "g_post_ffn", 16), last_low("in2", TU, "norm0", 16))

            def evacuate_in2(g):
                group_full("in2", g)
                r = over(rstd[:, 0:SEQ], 4)
                if g < 4:
                    ins = dve.scalar_tensor_tensor(qf[:, 4 * g:4 * g + 4, :], banks(g, 0, SEQ), HEAD ** -0.5, r,
                                                   ALU.mult, ALU.mult)
                else:
                    ins = dve.tensor_tensor((kf if g == 4 else vf)[:], banks(g, 0, SEQ), r, ALU.mult)
                ins.then_inc(group_read, 1)

            plain("in2", evacuate_in2, skip_first=True)
            dve.wait_ge(bias_landed, 16)
            dve.wait_ge(sinks_landed, 16)

            def head(i):
                g2, e, j = i // 8, i // 4 % 2, i % 4
                return 4 * (2 * g2 + e) + j

            def scores(i):
                s = i % SLOTS
                dve.wait_ge(s_ready, i + 1)
                if i >= SLOTS:
                    dve.wait_ge(p_ready, i - SLOTS + 1)
                rev = bias[:, head(i), ::-1]
                dve.tensor_tensor_reduce(sc[:, s, 0:QB], ps[:, i % 2, 0:QB], rev[:, QB:SEQ], 1.0, MASKED, ALU.add, ALU.max,
                                         rowmax[:, s, 0:1])
                dve.tensor_tensor_reduce(sc[:, s, QB:384], ps[:, i % 2, QB:384], rev, 1.0, MASKED, ALU.add, ALU.max,
                                         rowmax[:, s, 1:2]).then_inc(sc_ready, 1)
                dve.wait_ge(sc_ready, i + 1)
                dve.tensor_scalar(negmax[:, s], rowmax[:, s], sinks[:, head(i):head(i) + 1], -1.0, ALU.max,
                                  ALU.mult).then_inc(max_ready, 1)

            def normalise(i):
                s = i % SLOTS
                dve.wait_ge(p_ready, i + 1)
                dve.tensor_tensor(denom[:, s], rowsum[:, s], esink[:, s], ALU.add).then_inc(dve_step, 1)
                t = steps.add()
                dve.wait_ge(dve_step, t)
                dve.reciprocal(rdenom[:, s], denom[:, s]).then_inc(dve_step, 1)
                t = steps.add()
                dve.wait_ge(dve_step, t)
                dve.tensor_scalar(pr[:, s, 0:QB], pr[:, s, 0:QB], rdenom[:, s, 0:1], None, ALU.mult)
                dve.tensor_scalar(pr[:, s, QB:384], pr[:, s, QB:384], rdenom[:, s, 1:2], None, ALU.mult).then_inc(pn_ready, 1)

            def out_low(grp):
                g2, e = divmod(grp, 2)
                dve.wait_ge(o_high, 2 * grp + 2)
                rows = slice(64 * e, 64 * e + 64)
                for b in range(2):
                    dst = (slice(64 * e, 64 * e + 64), slice(4 * g2, 4 * g2 + 4), slice(b * QB, (b + 1) * QB))
                    dve.tensor_tensor(y2l[dst], ps[rows, 4 + 2 * (grp % 2) + b, :].rearrange("p (j q) -> p j q", j=4),
                                      y2h[dst].bitcast(F32), ALU.subtract).then_inc(o_low, 1)

            for i in range(N_HEADS + 8):
                if i < N_HEADS:
                    scores(i)
                if 2 <= i < N_HEADS + 2:
                    normalise(i - 2)
                if i >= 11 and (i - 11) % 4 == 0:
                    out_low((i - 11) // 4)
            plain("out2", mix_out("out2", mix2, SEQ))
            inverse_root("out2", rstd_post)
            dve.wait_ge(group_read, G0["up2"])
            opening("up2", residual_tile("up2", mix2, SEQ, TU, "norm1", 32), last_low("up2", TU, "norm2", 32))
            dve.memset(gt[:, :, 0:2], 0.0)
            feed_forward("up2", True)
            plain("down2", mix_out("down2", mixf, SEQ))
            inverse_root("down2", rstd_post)
            dve.wait_ge(group_read, G0["down2"] + 4)
            tile = residual_tile(None, mixf, SEQ, TU, "norm3", 48)
            for k in range(KT):
                tile(k)

        @block.tensor
        def _(pe):

            def group(name, g, parity, moving, n, before=None):
                per = CHUNKS[name]
                chunks_of(name, g * per + FIRST[name], (FIRST[name] + parity * per) % RING, parity, moving, n,
                          range(per), before)

            def chunks_of(name, n0, slot0, parity, moving, n, rows, before=None):
                per = CHUNKS[name]
                for c in rows:
                    pe.wait_ge(low_ready, n0 + (c - rows[0] + 1))
                    slot = (slot0 + c - rows[0]) % RING
                    for kk in range(2):
                        k = 2 * c + kk
                        if before:
                            before(k)
                        hi, lo = moving(k)
                        for m in range(4):
                            out = ps[:, 4 * parity + m, 0:n]
                            w_high, w_low = wh[:, slot, kk, m * P:(m + 1) * P], wl[:, slot, kk, m * P:(m + 1) * P]
                            pe.matmul(out, w_high, hi, start=(k == 0), stop=False)
                            pe.matmul(out, w_high, lo, start=False, stop=False)
                            last = pe.matmul(out, w_low, hi, start=False, stop=(k == 2 * per - 1))
                    last.then_inc(chunk_used, 1)

            def square_sum(name):
                output = name in OUTPUTS
                pe.wait_ge(sq_added, SQ0[name] + SQUARES[name])
                for b, col, t, n in sum_parts(name):
                    last = pe.matmul(ps[:, b, col:col + n], ones[:], sq_sum[:, t:t + n], start=True, stop=not output)
                if output:
                    n = TOKENS[name]
                    for k in range(4):
                        pe.wait_ge(last_sq, 4 * (OUTPUTS.index(name)) + k + 1)
                        last = pe.matmul(ps[:, 0, 0:n], ones[:], sq_last[:, k, 0:n], start=False, stop=(k == 3))
                last.then_inc(ss_done, 1)

            def whole(name, moving, n, before):
                for parity in range(2):
                    pe.wait_ge(group_read, G0[name] + parity - 1)
                    group(name, parity, parity, moving, n, None if parity else before)
                with pe.Fori(1, GROUPS[name] // 2) as i:
                    for parity in range(2):
                        pe.wait_ge(group_read, 2 * i + (G0[name] + parity - 1))
                        group(name, 2 * i + parity, parity, moving, n)
                square_sum(name)

            def x_of(n):
                return lambda k: (xh[:, k, 0:n], xl[:, k, 0:n])

            def tile_ready(name):
                return lambda k: pe.wait_ge(x_low, 16 * XSPLIT[name] + k + 1)

            group("w_in", 0, 0, x_of(L), L, tile_ready("w_in"))
            pe.wait_ge(consts, 16 * 6)
            square_sum("w_in")
            for b in range(2):
                last = pe.matmul(ps[0:32, 2 + b, L:L + 192], table[:], onehot[:, 192 * b:192 * (b + 1)], start=True, stop=True)
            last.then_inc(bias_mm, 1)
            group("w_in", 1, 1, x_of(L), L)
            with pe.Fori(1, 3) as i:
                for parity in range(2):
                    pe.wait_ge(group_read, 2 * i + (parity - 1))
                    group("w_in", 2 * i + parity, parity, x_of(L), L)
            pe.wait_ge(group_read, 5)
            group("w_in", 6, 0, x_of(L), L)

            def x_conv(k):
                return xh[:, k, TG - 2:L], xl[:, k, TG - 2:L]

            def per_tile(half, lhs, rhs, n, parts=1, upper_first=True):
                b = 4 * ((half + upper_first) % 2)
                for i in range(4):
                    f = 4 * half + i
                    for k in range(parts):
                        last = pe.matmul(ps[:, b + i, 0:n], lhs(f, k), rhs(f, k), start=(k == 0), stop=(k == parts - 1))
                last.then_inc(pre_pe, 1)

            pe.wait_ge(lora_landed, 16 * 6)
            pe.wait_ge(pre_act, 2)
            for half in range(2):
                pe.wait_ge(group_read, 6 + half)
                per_tile(half, lambda f, k: aup[:, f * P:(f + 1) * P], lambda f, k: z[0:LORA, 1, 1:L + 1], L)
            for half in range(2):
                pe.wait_ge(pre_act, 6 + 4 * half)
                per_tile(half, lambda f, k: wdu[:, f * P:(f + 1) * P], lambda f, k: tw[0:LORA, :], L)
            for g in (7, 8):
                pe.wait_ge(pre_act, 14 + 4 * (g - 7))
                group("w_in", g, g % 2, x_conv, L - TG + 2)
            pe.wait_ge(pre_act, 19)
            for half in range(2):
                pe.wait_ge(group_read, 8 + half)
                per_tile(half, lambda f, k: bones[:], lambda f, k: rkr[:, f, :], L)
            for g in range(9, 13):
                if g < 11:
                    pe.wait_ge(pre_act, 20 + (g - 9))
                else:
                    pe.wait_ge(group_read, g - 1)
                group("w_in", g, g % 2, x_conv, L - TG + 2)
            for half in range(2):
                pe.wait_ge(group_read, 12 + half)
                per_tile(half, lambda f, k: gup[:, k, f * P:(f + 1) * P], lambda f, k: sgd[:, k, :], L, 2)
            pe.wait_ge(pre_dve, 2)
            for half in range(2):
                pe.wait_ge(pre_act, 22 + half)
                per_tile(half, lambda f, k: bones[:], lambda f, k: rkr[:, f, :], L)
            pe.wait_ge(pre_dve, 7)

            def batch(b, half, lhs, rhs, done):
                for i in range(HALF_TILES):
                    f = HALF_TILES * half + i
                    last = pe.matmul(ps[:, b, P * i:P * (i + 1)], lhs(f), rhs(f), start=True, stop=True)
                last.then_inc(done, 1)

            def two_terms(b, half, terms, done):
                for i in range(HALF_TILES):
                    f = HALF_TILES * half + i
                    for x, (lhs, rhs) in enumerate(terms):
                        last = pe.matmul(ps[:, b, P * i:P * (i + 1)], lhs(f), rhs(f), start=(x == 0), stop=(x == len(terms) - 1))
                last.then_inc(done, 1)

            def join(c, l, half):
                pe.wait_ge(q_ready, inner(c, l, half))
                if l < LEVELS[c] - 1:
                    for i in range(HALF_TILES):
                        f = HALF_TILES * half + i
                        pe.matmul(ps[:, 2 + half, P * i:P * (i + 1)], tt[:, f, :], qb[:, f, :], start=True, stop=True)
                batch(4 + half, half, lambda f: qb[:, f, :], lambda f: tt[:, f, :], d_done)

            def product(c, l, half):
                pe.wait_ge(am_ready, level(c, l, half))
                pe.wait_ge(tt_ready, level(c, l - 1, half))
                batch(half, half, lambda f: am[l % 2][:, f, :], lambda f: tn[:, f, :], q_done)

            for c in range(N_RC + 1):
                p = c - 1
                xp, arp, grp = xuv[p % 2], ar[p % 2], gr[p % 2]
                if c < N_RC:
                    pe.wait_ge(fac_ready, c + 1)
                    pe.wait_ge(bk_ready, 4 * c + 4)
                    if c:
                        pe.wait_ge(tt_ready, level(p, LEVELS[p] - 1))
                    for half in range(2):
                        for i in range(HALF_TILES):
                            f = HALF_TILES * half + i
                            for e in range(2):
                                last = pe.matmul(ps[:, 2 * e + half, P * i:P * (i + 1)], bkf[HEAD_ROWS[e], f, :],
                                                 ar[c % 2][HEAD_ROWS[e], f, 64:192], start=True, stop=True)
                        last.then_inc(gram_done, 1)
                if c:
                    pe.wait_ge(v_ready, 4 * c)
                    for half in range(2):
                        if p:
                            pe.wait_ge(st_ready, nth(p - 1, half))
                        terms = [(lambda f: ga[:, f, :], lambda f: xp[:, f, :]),
                                 (lambda f: arp[:, f, 0:P], lambda f: st[:, f, :])]
                        two_terms(6 + half, half, terms if p else terms[:1], z_done)
                if c < N_RC:
                    for half in range(2):
                        for i in range(HALF_TILES):
                            last = pe.transpose(ps[:, 4 + half, P * i:P * (i + 1)], bkf[:, HALF_TILES * half + i, :], ident[:])
                        last.then_inc(bk_turned, 1)
                if c:
                    if c == N_RC:
                        pe.wait_ge(tt_ready, level(p, LEVELS[p] - 1))
                    for half in range(2):
                        pe.wait_ge(zb_ready, nth(p, half))
                        batch(6 + half, half, lambda f: tt[:, f, :], lambda f: zb[:, f, :], u_done)
                    for half in range(2):
                        pe.wait_ge(x_ready, 2 * nth(p, half))
                        if c < N_RC:
                            batch(6 + half, half, lambda f: bkt[:, f, :], lambda f: xp[:, f, :], s_done)
                    for half in range(2):
                        if c < N_RC:
                            pe.wait_ge(am_ready, level(c, 0, half))
                        terms = [(lambda f: xp[:, f, :], lambda f: grp[:, f, :]),
                                 (lambda f: st[:, f, :], lambda f: arp[:, f, P:2 * P])]
                        two_terms(half, half, terms if p else terms[:1], y_done)
                if c == N_RC:
                    continue
                pe.wait_ge(vd_ready, c + 1)
                for half in range(2):
                    pe.wait_ge(bkt_ready, nth(c, half))
                    for i in range(HALF_TILES):
                        last = pe.transpose(ps[:, 4 + half, P * i:P * (i + 1)], vd[:, HALF_TILES * half + i, :], ident[:])
                    last.then_inc(v_done, 1)
                for half in range(2):
                    pe.wait_ge(am_ready, level(c, 0, half))
                    batch(2 + half, half, lambda f: am[0][:, f, :], lambda f: ident[:], am_turned)
                if c:
                    pe.wait_ge(y_ready, 4 * c)
                pe.wait_ge(v_ready, 4 * c + 4)
                for l in range(1, LEVELS[c]):
                    product(c, l, 0)
                    if l > 1:
                        join(c, l - 1, 1)
                    join(c, l, 0)
                    product(c, l, 1)
                join(c, LEVELS[c] - 1, 1)
            pe.wait_ge(y_ready, 4 * N_RC)
            for f in range(RT):
                last = pe.matmul(ps[:, f, 0:LG], bones[:], z[:, 4 + f, 1 + TG:1 + L], start=True, stop=True)
            last.then_inc(pre_pe, 1)
            pe.wait_ge(pre_act, 24)
            for half in range(2):
                per_tile(half, lambda f, k: bones[:], lambda f, k: yc2[:, f, :], LG, upper_first=False)

            def y_of(k):
                if k < RT:
                    return ych[:, k, :], ycl[:, k, :]
                return yrh[:, k - RT, :], yrl[:, k - RT, :]

            pe.wait_ge(y_low, 2)
            for g, c0 in ((0, 0), (1, 0), (0, 4), (1, 4)):
                if c0 == 0:
                    pe.wait_ge(pre_act, 25 + g)
                    before = None
                else:
                    before = lambda k: pe.wait_ge(y_low, 3 + (k - RT) // 4)
                chunks_of("w_out", FIRST["w_out"] + 2 * c0 + 4 * g, 0, g, y_of, LG, range(c0, c0 + 4), before)
            with pe.Fori(1, 2) as i:
                for parity in range(2):
                    pe.wait_ge(group_read, 2 * i + (G0["w_out"] + parity - 1))
                    group("w_out", 2 * i + parity, parity, y_of, LG)
            square_sum("w_out")

            def feed_forward(name):
                n = TOKENS[name]
                r0 = G0[name]

                def x_up(k):
                    return (xh[:, k, n - SEQ:n], xl[:, k, n - SEQ:n])

                group(name, 0, 0, x_of(n), n, tile_ready(name))
                square_sum(name)
                group(name, 1, 1, x_up, SEQ)
                with pe.Fori(1, PAIRS) as p:
                    pe.wait_ge(group_read, 2 * p + (r0 - 1))
                    group(name, 2 * p, 0, x_of(n), n)
                    pe.wait_ge(group_read, 2 * p + r0)
                    group(name, 2 * p + 1, 1, x_up, SEQ)

            def down(name, p0):
                whole(name, lambda k: (acth[:, k, :], actl[:, k, :]), SEQ,
                      lambda k: pe.wait_ge(act_low, p0 + k // 4 + 1))

            feed_forward("gate_up")
            down("down", 0)

            group("in2", 0, 0, x_of(SEQ), SEQ, tile_ready("in2"))
            square_sum("in2")
            group("in2", 1, 1, x_of(SEQ), SEQ)
            with pe.Fori(1, 3) as i:
                pe.wait_ge(group_read, 2 * i + (G0["in2"] - 1))
                group("in2", 2 * i, 0, x_of(SEQ), SEQ)
                pe.wait_ge(group_read, 2 * i + G0["in2"])
                group("in2", 2 * i + 1, 1, x_of(SEQ), SEQ)

            pe.wait_ge(group_read, G0["out2"])
            for kb in range(2):
                for g2 in range(4):
                    last = pe.transpose(ps[:, kb, P * g2:P * (g2 + 1)], vf[:, g2, QB * kb:QB * (kb + 1)], ident[:])
            last.then_inc(v_turned, 1)
            pe.wait_ge(vt_ready, 1)

            def scores(i):
                g2, e, j = i // 8, i // 4 % 2, i % 4
                rows = slice(64 * e, 64 * e + 64)
                if i >= 2:
                    pe.wait_ge(sc_ready, i - 1)
                pe.matmul(ps[:, i % 2, 0:QB], qf[rows, 4 * g2 + j, 0:QB], kf[rows, g2, 0:QB], start=True, stop=True)
                pe.matmul(ps[:, i % 2, QB:384], qf[rows, 4 * g2 + j, QB:SEQ], kf[rows, g2, 0:SEQ], start=True,
                          stop=True).then_inc(s_ready, 1)

            def turn(i):
                pe.wait_ge(pn_ready, i + 1)
                if i >= 2:
                    pe.wait_ge(pt_ready, i - 1)
                for t in range(3):
                    last = pe.transpose(ps[:, 2 + i % 2, QB * t:QB * (t + 1)], pr[:, i % SLOTS, QB * t:QB * (t + 1)], ident[:])
                last.then_inc(p_turned, 1)

            def values(grp):
                g2, e = divmod(grp, 2)
                rows = slice(64 * e, 64 * e + 64)
                pe.wait_ge(pt_ready, 4 * grp + 4)
                if grp >= 2:
                    pe.wait_ge(o_low, 2 * (grp - 1))
                bank = 4 + 2 * (grp % 2)
                v = [vt[:, kb, P * g2 + 64 * e:P * g2 + 64 * e + 64] for kb in range(2)]
                for b, terms in enumerate((((0, 0),), ((0, 1), (1, 2)))):
                    for x, (kb, t) in enumerate(terms):
                        last = pe.matmul(ps[rows, bank + b, :], v[kb], pt[:, grp % 2, t, :, :].rearrange("p j q -> p (j q)"),
                                         start=(x == 0), stop=(x == len(terms) - 1))
                last.then_inc(o_done, 1)

            for i in range(N_HEADS + 5):
                if i < N_HEADS:
                    scores(i)
                if 3 <= i < N_HEADS + 3:
                    turn(i - 3)
                if i >= 8 and (i - 8) % 4 == 0:
                    values((i - 8) // 4)

            pe.wait_ge(o_low, 16)
            whole("out2", lambda k: (y2h[:, k, :], y2l[:, k, :]), SEQ, None)
            feed_forward("up2")
            down("down2", PAIRS)



def _features(v):
    return np.asarray(v).reshape(-1, P).T


def _chunks(w):
    rows, cols = w.shape
    w = w.reshape(rows // 256, 2, P, cols // 512, 512)
    return np.ascontiguousarray(w.transpose(3, 0, 2, 1, 4)).reshape(-1, P, 2, 512)


def _pad(w, axis, n):
    widths = [(0, 0)] * w.ndim
    widths[axis] = (0, n)
    return np.pad(w, widths)


def _lora_parts(v, axis):
    a, b, c = np.split(v, [LORA, 2 * LORA], axis=axis)
    return [_pad(a, axis, P - LORA), _pad(b, axis, P - LORA), c]


def _constants():
    i = np.arange(P)
    same_head = (i[:, None] // C == i[None, :] // C).astype(np.float32)
    src, dst = i[:, None] % C, i[None, :] % C
    lmask = np.stack([same_head * (src // (2 * m) == dst // (2 * m)) * (src % (2 * m) < m) * (dst % (2 * m) >= m)
                      for m in (1, 2, 4, 8, 16, 32)], axis=1)
    t = np.arange(C)[None, :]
    gmask = np.stack([(i[:, None] % C) < t, (i[:, None] % C) <= t], axis=1)
    reset = np.ones((P, L))
    reset[:, 0:L:C] = 0.0
    dist = np.arange(384) - (QB - 1)
    ok = (dist >= 0) & (dist < QB)
    near = np.maximum(dist, 0)
    far = np.log(np.maximum(near, 1).astype(np.float32) / np.float32(16)) / np.float32(math.log(8.0))
    bucket = np.where(near < 16, near, np.minimum(16 + (far * 16).astype(np.int32), 31))
    onehot = (np.arange(32)[:, None] == bucket[None, :]) & ok[None, :]
    maskrow = np.broadcast_to(np.where(ok, 0.0, MASKED), (32, 384))
    return {"ident": np.eye(P), "ones": np.ones((P, P)), "bones": same_head, "lmask": lmask, "gmask": gmask,
            "reset": reset, "onehot": onehot, "maskrow": maskrow}


_OUT = (P, KT, SEQ)


def kernel(**inputs):
    import concourse.bacc as bacc
    from concourse.bass_utils import run_bass_kernel_spmd

    a = {k: np.asarray(v) for k, v in inputs.items()}
    hidden = np.concatenate([a["meta_tokens"], a["x"][0]], axis=0)
    conv, rwkv = a["w_in"][:, :3 * RW], a["w_in"][:, 3 * RW:]
    gate_b, gate_c, hx = np.split(conv, 3, axis=1)
    columns = _lora_parts(rwkv[:, 3 * RW:], 1) + [rwkv[:, :3 * RW]]
    for half in range(2):
        cut = slice(512 * half, 512 * half + 512)
        columns += [gate_c[:, cut], hx[:, cut], gate_b[:, cut]]
    gate, up = np.split(a["w_gate_up"], 2, axis=1)
    gate_up = np.stack([gate.reshape(D, -1, 512), up.reshape(D, -1, 512)], axis=2).reshape(D, -1)
    up2 = a["ffn_w_up_2"][0].reshape(D, 2, -1, 512).transpose(0, 2, 1, 3).reshape(D, -1)
    heads = a["swa_w_in_2"][0][:, :D].reshape(D, 4, 2, 4, HEAD).transpose(0, 1, 3, 2, 4).reshape(D, D)
    in2 = np.concatenate([heads, a["swa_w_in_2"][0][:, D:]], axis=1)
    out2 = a["swa_w_out_2"][0].reshape(4, 2, 4, HEAD, D).transpose(0, 2, 1, 3, 4).reshape(D, D)
    mu = np.concatenate(_lora_parts(a["mu_rwkv"][3 * RW:], 0) + [a["mu_rwkv"][:3 * RW]])
    vectors = [a["g_pre_mix"], a["g_post_mix"], a["g_pre_ffn"], a["g_post_ffn"], *a["norm_g_2"][0], mu, a["w0"], a["a0"],
               a["k_k"], a["k_a"], a["r_k"].reshape(-1), a["ln_x_w"], a["ln_x_b"], a["conv_w"].reshape(-1),
               a["conv_ffn"].reshape(-1), a["ffn_conv_2"][0].reshape(-1)]
    w_out = _chunks(a["w_out"])
    w_out = w_out[np.r_[0:4, 8:12, 4:8, 12:32]]
    arrays = {
        "ht": hidden.T.reshape(KT, P, L).transpose(1, 0, 2),
        "w_in": _chunks(np.concatenate(columns, axis=1)), "w_out": w_out, "gate_up": _chunks(gate_up),
        "down": _chunks(a["w_down"]), "in2": _chunks(in2), "out2": _chunks(out2), "up2": _chunks(up2),
        "down2": _chunks(a["ffn_w_down_2"][0]),
        "vec": np.concatenate([_features(v) for v in vectors], axis=1),
        "wdu": a["w_decay_up"], "aup": a["a_up"], "gup": a["g_up"].reshape(2, P, RW).transpose(1, 0, 2),
        "table": a["rel_bias_table_2"], "sinks": np.broadcast_to(a["swa_sinks_2"][0], (P, N_HEADS)),
        **{k: np.asarray(v, np.float32) for k, v in _constants().items()},
    }
    nc = bacc.Bacc("TRN2", target_bir_lowering=False, num_devices=1, dynamic_dma_scratch_size=1024)
    named, d = {}, {}
    for name, v in arrays.items():
        v = np.ascontiguousarray(v)
        named[f"in_{name}"] = v
        d[name] = nc.dram_tensor(f"in_{name}", v.shape, mybir.dt.from_np(v.dtype), kind="ExternalInput").ap()
    d["out"] = nc.dram_tensor("out_0", _OUT, F32, kind="ExternalOutput").ap()
    program(nc, d)
    out = run_bass_kernel_spmd(nc, [named], core_ids=[0]).results[0]["out_0"]
    return np.ascontiguousarray(out.transpose(1, 0, 2).reshape(D, SEQ).T)[None]
```
